# Optimizing a Trainium2 kernel written in Bass

```python
import jax, jax.numpy as jnp
from jax import lax
import numpy as np

D_MODEL = 1024
BATCH = 1
SEQ = 512
DEPTH = 2

GRID_W = 64
CTX_LEN = 256
N_MIXERS = 2
NA_HEADS = 16
NA_HEAD_DIM = D_MODEL // NA_HEADS
WIN_R = 8
WIN_C = 16
FNO_GROUPS = 4
FNO_GROUP_DIM = D_MODEL // FNO_GROUPS
PEER_HEADS = 8
PEER_N_KEYS = 128
PEER_N_EXPERTS = PEER_N_KEYS * PEER_N_KEYS
PEER_TOPK = 16
PEER_KEY_DIM = 256
PEER_HALF = PEER_KEY_DIM // 2
PEER_BLOCK = 128
N_MOD = 6
EPS = 1e-6

kernel_name = "hybrid_na_fnet_peer_dit"

def rmsnorm(x, g):
    xf = x.astype(jnp.float32)
    y = xf * lax.rsqrt(jnp.mean(xf * xf, axis=-1, keepdims=True) + EPS)
    return y.astype(x.dtype) * g

def split_heads(t):
    return t.reshape(t.shape[0], t.shape[1], NA_HEADS, NA_HEAD_DIM)

def neighbourhood_attention(q, k, v, k_ctx, v_ctx, rpb):
    b, n, h, dh = q.shape
    rows = n // GRID_W
    kr = min(WIN_R, rows)
    kc = min(WIN_C, GRID_W)
    scale = dh ** -0.5
    qg = q.reshape(b, rows, GRID_W, h, dh)
    kg = k.reshape(b, rows, GRID_W, h, dh)
    vg = v.reshape(b, rows, GRID_W, h, dh)
    col = jnp.arange(GRID_W)
    c_start = jnp.clip(col - kc // 2, 0, GRID_W - kc)
    in_win = (col[None, :] >= c_start[:, None]) & (col[None, :] < c_start[:, None] + kc)
    dc_idx = jnp.clip(col[None, :] - col[:, None] + WIN_C - 1, 0, 2 * WIN_C - 2)
    rpb_f = rpb.astype(jnp.float32)
    neg = jnp.finfo(jnp.float32).min

    def row_block(r):
        r_start = jnp.clip(r - kr // 2, 0, rows - kr)
        q_r = lax.dynamic_index_in_dim(qg, r, axis=1, keepdims=False)
        k_r = lax.dynamic_slice_in_dim(kg, r_start, kr, axis=1)
        v_r = lax.dynamic_slice_in_dim(vg, r_start, kr, axis=1)
        dr_idx = r_start + jnp.arange(kr) - r + WIN_R - 1
        bias = rpb_f[:, dr_idx][:, :, dc_idx].transpose(0, 2, 1, 3)
        s_lat = jnp.einsum('bqhd,bikhd->bhqik', q_r, k_r).astype(jnp.float32) * scale + bias[None]
        s_lat = jnp.where(in_win[:, None, :], s_lat, neg)
        s_ctx = jnp.einsum('bqhd,bchd->bhqc', q_r, k_ctx).astype(jnp.float32) * scale
        s = jnp.concatenate([s_lat.reshape(b, h, GRID_W, kr * GRID_W), s_ctx], axis=-1)
        p = jax.nn.softmax(s, axis=-1).astype(v.dtype)
        p_lat = p[..., :kr * GRID_W].reshape(b, h, GRID_W, kr, GRID_W)
        p_ctx = p[..., kr * GRID_W:]
        return (jnp.einsum('bhqik,bikhd->bqhd', p_lat, v_r)
                + jnp.einsum('bhqc,bchd->bqhd', p_ctx, v_ctx))

    out = lax.map(row_block, jnp.arange(rows))
    return out.transpose(1, 0, 2, 3, 4).reshape(b, n, h * dh)

def context_attention(q, k, v):
    b, cl, h, dh = q.shape
    s = jnp.einsum('bqhd,bkhd->bhqk', q, k).astype(jnp.float32) * dh ** -0.5
    p = jax.nn.softmax(s, axis=-1).astype(v.dtype)
    return jnp.einsum('bhqk,bkhd->bqhd', p, v).reshape(b, cl, h * dh)

def fourier_mix(h, w_out):
    b, n, d = h.shape
    hg = h.astype(jnp.float32).reshape(b, n, FNO_GROUPS, FNO_GROUP_DIM)
    f = jnp.fft.fftn(hg, axes=(1, 3), norm="ortho").real
    return f.reshape(b, n, d).astype(h.dtype) @ w_out

def peer_ffn(h, w_query, sub_keys, u_tab, v_tab):
    b, n, d = h.shape
    xb = h.reshape(-1, PEER_BLOCK, d)

    def block(xt):
        t = xt.shape[0]
        q = (xt @ w_query).reshape(t, PEER_HEADS, 2, PEER_HALF)
        s = jnp.einsum('thpk,pek->thpe', q, sub_keys).astype(jnp.float32)
        s_a, i_a = lax.top_k(s[:, :, 0], PEER_TOPK)
        s_b, i_b = lax.top_k(s[:, :, 1], PEER_TOPK)
        cand_s = (s_a[..., :, None] + s_b[..., None, :]).reshape(t, PEER_HEADS, PEER_TOPK * PEER_TOPK)
        cand_i = (i_a[..., :, None] * PEER_N_KEYS + i_b[..., None, :]).reshape(t, PEER_HEADS, PEER_TOPK * PEER_TOPK)
        top_s, pos = lax.top_k(cand_s, PEER_TOPK)
        idx = jnp.take_along_axis(cand_i, pos, axis=-1)
        g = jax.nn.softmax(top_s, axis=-1).astype(xt.dtype)
        act = jax.nn.gelu(jnp.einsum('thkd,td->thk', u_tab[idx], xt), approximate=False)
        return jnp.einsum('thk,thkd->td', g * act, v_tab[idx])

    return lax.map(block, xb).reshape(b, n, d)

def setup_inputs(seed: int = 0) -> dict:
    key = jax.random.key(seed)
    ks = jax.random.split(key, 17)
    n_na = (DEPTH + N_MIXERS - 1) // N_MIXERS
    n_fno = DEPTH // N_MIXERS
    D = D_MODEL

    def nrm(k, shape, s):
        return jax.random.normal(k, shape, jnp.float32) * s

    return {
        "x": nrm(ks[0], (BATCH, SEQ, D), 1.0),
        "c": nrm(ks[1], (BATCH, D), 1.0),
        "ctx": nrm(ks[2], (BATCH, CTX_LEN, D), 1.0),
        "c_ctx": nrm(ks[3], (D,), 1.0),
        "norm_mix": 1.0 + nrm(ks[4], (DEPTH, D), 0.02),
        "norm_ffn": 1.0 + nrm(ks[5], (DEPTH, D), 0.02),
        "w_mod": nrm(ks[6], (DEPTH, D, N_MOD * D), 0.5 * D ** -0.5),
        "b_mod": nrm(ks[7], (DEPTH, N_MOD * D), 0.02),
        "na_w_qkv": nrm(ks[8], (n_na, D, 3 * D), D ** -0.5),
        "na_w_o": nrm(ks[9], (n_na, D, D), D ** -0.5),
        "na_rpb": nrm(ks[10], (n_na, NA_HEADS, 2 * WIN_R - 1, 2 * WIN_C - 1), 0.5),
        "fno_w_out": nrm(ks[11], (n_fno, D, D), D ** -0.5),
        "peer_w_query": nrm(ks[12], (DEPTH, D, PEER_HEADS * PEER_KEY_DIM), D ** -0.5),
        "peer_sub_keys": nrm(ks[13], (DEPTH, 2, PEER_N_KEYS, PEER_HALF), PEER_HALF ** -0.5),
        "peer_u": nrm(ks[14], (DEPTH, PEER_N_EXPERTS, D), D ** -0.5),
        "peer_v": nrm(ks[15], (DEPTH, PEER_N_EXPERTS, D), 1.0),
        "norm_final": 1.0 + nrm(ks[16], (D,), 0.02),
    }

def reference(x, c, ctx, c_ctx, norm_mix, norm_ffn, w_mod, b_mod, na_w_qkv, na_w_o, na_rpb,
              fno_w_out, peer_w_query, peer_sub_keys, peer_u, peer_v, norm_final):
    xc = ctx
    for i in range(DEPTH):
        mixer = i % N_MIXERS
        j = i // N_MIXERS
        ctx_read_later = any(l % N_MIXERS == 0 for l in range(i + 1, DEPTH))
        need_ctx_in = ctx_read_later or mixer == 0

        mod_x = jax.nn.silu(c) @ w_mod[i] + b_mod[i]
        sh_m, sc_m, g_m, sh_f, sc_f, g_f = jnp.split(mod_x[:, None, :], N_MOD, axis=-1)
        hx = rmsnorm(x, norm_mix[i]) * (1 + sc_m) + sh_m
        if need_ctx_in:
            mod_c = jax.nn.silu(c_ctx) @ w_mod[i] + b_mod[i]
            csh_m, csc_m, cg_m, csh_f, csc_f, cg_f = jnp.split(mod_c, N_MOD, axis=-1)
            hc = rmsnorm(xc, norm_mix[i]) * (1 + csc_m) + csh_m

        if mixer == 0:
            q, k, v = jnp.split(hx @ na_w_qkv[j], 3, axis=-1)
            k_c, v_c = jnp.split(hc @ na_w_qkv[j][:, D_MODEL:], 2, axis=-1)
            k_c, v_c = split_heads(k_c), split_heads(v_c)
            mix_x = neighbourhood_attention(split_heads(q), split_heads(k), split_heads(v),
                                            k_c, v_c, na_rpb[j]) @ na_w_o[j]
            if ctx_read_later:
                q_c = split_heads(hc @ na_w_qkv[j][:, :D_MODEL])
                mix_c = context_attention(q_c, k_c, v_c) @ na_w_o[j]
        else:
            mix_x = fourier_mix(hx, fno_w_out[j])
            if ctx_read_later:
                mix_c = fourier_mix(hc, fno_w_out[j])

        x = x + g_m * mix_x
        hx = rmsnorm(x, norm_ffn[i]) * (1 + sc_f) + sh_f
        x = x + g_f * peer_ffn(hx, peer_w_query[i], peer_sub_keys[i], peer_u[i], peer_v[i])
        if ctx_read_later:
            xc = xc + cg_m * mix_c
            hc = rmsnorm(xc, norm_ffn[i]) * (1 + csc_f) + csh_f
            xc = xc + cg_f * peer_ffn(hc, peer_w_query[i], peer_sub_keys[i], peer_u[i], peer_v[i])
    return rmsnorm(x, norm_final)


_drawn_inputs = setup_inputs


def setup_inputs(seed=0):
    import zlib

    import numpy as np

    out = dict(_drawn_inputs(seed))
    spreads = {}
    factors = {'norm_mix': 3.515, 'norm_final': 2.858}
    for name, (base, spread) in spreads.items():
        noise = np.random.default_rng([zlib.crc32(name.encode()), seed]).standard_normal(out[name].shape)
        drawn = base * np.exp(spread * noise) if base else spread * noise
        out[name] = __import__('jax').numpy.asarray(drawn.astype(out[name].dtype))
    for name, factor in factors.items():
        out[name] = (out[name] * factor).astype(out[name].dtype)
    return out
```

```python
from contextlib import ExitStack

import numpy as np
import concourse.bass as bass
from concourse import mybir

ALU = mybir.AluOpType
ACT = mybir.ActivationFunctionType
AX = mybir.AxisListType
F32 = mybir.dt.float32
U32 = mybir.dt.uint32

P = 128
D = 1024
KD = D // P
SEQ = 512
NT = SEQ // P
CTX = 256
NC = CTX // P
GRID_W = 64
ROWS = SEQ // GRID_W
HEADS = 16
PAIRS = HEADS // 2
DH = D // HEADS
WIN_C = 16
COLS_T = P // ROWS
WIN = 256
DEPTH = 2
N_MOD = 6
MODB = N_MOD * KD
PH = 8
NKEY = 128
TOPK = 16
G = 8
NPAIR_T = PH // 2
KSTEPS = 12
EPS = 1e-6
NEG = -3.0e38
BIG = 512
SLOTS = 4
WSTART = [min(max(P * b - WIN // 4, 0), SEQ - WIN) for b in range(NT)]
VARIANT = [0, 1, 1, 2]
SHIFT = [WIN_C - 1, WIN_C - 1 - 8, WIN_C - 1 - 16]
PADC = 16
LENC = 64


def hold(eng, sem, value):
    eng.wait_ge(sem, value)
    eng.nop(nofuse=True)


class Count:

    def __init__(self, eng, sem, base=0):
        self.eng, self.sem, self.base, self.n = eng, sem, base, 0

    def sig(self, ins):
        self.n += 1
        ins.then_inc(self.sem, 1)

    def wait(self):
        if isinstance(self.base, int):
            self.eng.wait_ge(self.sem, self.base + self.n)
        else:
            hold(self.eng, self.sem, self.base + self.n)

    def step(self, ins):
        self.sig(ins)
        self.wait()


def build(nc, x, cT, ctx_in, normT, w_mod, bmodT, w_qkv, w_o, bias_tab, masks, w_fno, w_query, keysT,
          peer_u0, peer_u1, peer_v0, peer_v1, norm_fin, dft_ch, dft_pos, ident_in, iota_in, out):
    peer_u, peer_v = [peer_u0, peer_u1], [peer_v0, peer_v1]
    with ExitStack() as ctx:
        def sb(name, shape, dt=F32):
            return ctx.enter_context(nc.sbuf_tensor(name, shape, dt))

        def sem(name):
            return ctx.enter_context(nc.semaphore(name))

        r1 = sb("r1", [P, 16384])
        r2 = sb("r2", [P, 16384])
        r3 = sb("r3", [P, 6144])
        r5 = sb("r5", [P, 4096])
        xres = sb("xres", [P, NT, D])
        modb = sb("modb", [P, 4, D])
        AF, SHF, GF, GM = range(4)

        ring = r1[:, :].rearrange("p (s k n) -> p s k n", s=SLOTS, k=KD)
        urows = r1[:, 0:G * D].rearrange("p (g d) -> p g d", g=G)
        vrows = r1[:, G * D:2 * G * D].rearrange("p (g d) -> p g d", g=G)
        scratch = r1[:, 0:8192]
        qfix = [scratch[:, 0:128], scratch[:, 128:256]]
        p_mid = [scratch[:, 256 + 640 * i:256 + 640 * (i + 1)] for i in range(2)]
        p_edge = [scratch[:, 1536 + 512 * i:1536 + 512 * (i + 1)] for i in range(2)]
        pT = [scratch[:, 2560 + 640 * i:2560 + 640 * (i + 1)] for i in range(2)]
        qpair = scratch[:, 3840:3968]
        attn = scratch[:, 4096:5120]
        attnT = scratch[:, 5120:6144].rearrange("p (k n) -> p k n", k=KD)
        otmp = scratch[:, 6144:7168]
        sqj = scratch[:, 7168:8192]
        hT = r2[:, 0:4096].rearrange("p (k n) -> p k n", k=KD)
        hcT = r2[:, 4096:6144].rearrange("p (k n) -> p k n", k=KD)
        qT = r2[:, 6144:10240].rearrange("p (k n) -> p k n", k=KD)
        kT = r2[:, 10240:14336].rearrange("p (k n) -> p k n", k=KD)
        kcT = r2[:, 14336:16384].rearrange("p (k n) -> p k n", k=KD)
        vtok = r3[:, :].rearrange("p (t n) -> p t n", t=NT + NC)
        xctx = vtok[:, NT:NT + NC, :]
        xn = r5[:, :].rearrange("p (t n) -> p t n", t=NT)
        bias_a = r5[:, :].rearrange("p (h n) -> p h n", h=HEADS)
        bias_b = r2[:, 0:4096].rearrange("p (h n) -> p h n", h=HEADS)
        bias = [bias_a, bias_b, bias_a]
        masks_sb = r2[:, 4096:4096 + 3 * WIN].rearrange("p (v n) -> p v n", v=3)
        cs = r2[:, 4096:12288].rearrange("p (t g n) -> p t g n", t=NT, g=4)
        fT = r2[:, 12288:16384].rearrange("p (k n) -> p k n", k=KD)
        wq = r2[:, :].rearrange("p (k n) -> p k n", k=KD)
        hx_next, hx_cur = r5[:, 0:1024], r5[:, 1024:2048]
        hxT = r5[:, 2048:3072].rearrange("p (k n) -> p k n", k=KD)
        ytmp = r5[:, 3072:4096]
        diag = r3[:, 0:1024].rearrange("p (g n) -> p g n", g=G)
        q_sb = r3[:, 1024:1280]
        qT_sb = r3[:, 1280:1536].rearrange("p (a n) -> p a n", a=2)
        wk = r3[:, 1536:1792].rearrange("p (a n) -> p a n", a=2)
        cand = r3[:, 1792:2048]
        cand2 = r3[:, 2048:2304]
        onehot = r3[:, 2304:2816]
        topv = r3[:, 2816:2848].rearrange("p (a n) -> p a n", a=2)
        tab = r3[:, 2848:2880].rearrange("p (a n) -> p a n", a=2)
        tops = r3[:, 2880:2896]
        ftile = r3[:, 3072:4096]

        ident = sb("ident", [P, P])
        ones = sb("ones", [P, P])
        iota16 = sb("iota16", [P, TOPK + 2])
        keys = sb("keys", [P, DEPTH, 2, NKEY])
        craw = sb("craw", [P, KD, 2])
        silu = sb("silu", [P, KD, 2])
        norms = sb("norms", [P, 2 * DEPTH, KD])
        bmod = sb("bmod", [P, DEPTH, MODB])
        modc = sb("modc", [P, MODB, 2])
        a_mix = sb("a_mix", [P, KD, 2])
        a_ffn = sb("a_ffn", [P, KD])
        ss = sb("ss", [P, NT + NC])
        rstd = sb("rstd", [P, NT + NC])
        nmx = sb("nmx", [P, 2])
        esum = sb("esum", [P, HEADS])
        einv = sb("einv", [P, HEADS])
        ixu = sb("ixu", [P, 2, TOPK], U32)
        pos = sb("pos", [P, TOPK], U32)
        poshl = sb("poshl", [P, TOPK, 2], U32)
        idx = [sb(f"idx{i}", [P, TOPK], U32) for i in range(2)]
        gate_e = [sb(f"gate_e{i}", [P, TOPK]) for i in range(2)]
        gate_r = [sb(f"gate_r{i}", [P, 1]) for i in range(2)]
        expert = sb("expert", [P, TOPK])
        gsum = sb("gsum", [P, 1])
        gneg = sb("gneg", [P, 1])
        pre = sb("pre", [P, 2, G])
        gel = sb("gel", [P, 2, G])
        wgt = sb("wgt", [P, 2, G])
        ps = ctx.enter_context(nc.psum_tensor("ps", [P, 8, 512], F32))

        s_small = sem("s_small")
        s_x = sem("s_x")
        s_ctxin = sem("s_ctxin")
        s_bias = [sem(f"s_bias{v}") for v in range(3)]
        s_maskin = sem("s_maskin")
        s_out = sem("s_out")
        w_in = [[sem(f"w_in{L}_{i}") for i in range(SLOTS)] for L in range(DEPTH)]
        w_free = [sem(f"w_free{L}") for L in range(DEPTH)]
        wq_in = [sem(f"wq_in{L}") for L in range(DEPTH)]
        wfin_in = sem("wfin_in")
        s_ones = sem("s_ones")
        s_silu = sem("s_silu")
        sq_done = [sem(f"sq_done{L}") for L in range(DEPTH)]
        var_ok = [sem(f"var_ok{L}") for L in range(DEPTH)]
        std_ok = [sem(f"std_ok{L}") for L in range(DEPTH)]
        rstd_ok = [sem(f"rstd_ok{L}") for L in range(DEPTH)]
        xn_ok = [sem(f"xn_ok{L}") for L in range(DEPTH)]
        mod_ok = [sem(f"mod_ok{L}") for L in range(DEPTH)]
        dg_ok = [sem(f"dg_ok{L}") for L in range(DEPTH)]
        job = [sem(f"job{L}") for L in range(DEPTH)]
        ev_act = [sem(f"ev_act{L}") for L in range(DEPTH)]
        ev_dve = [sem(f"ev_dve{L}") for L in range(DEPTH)]
        dchain = [sem(f"dchain{L}") for L in range(DEPTH)]
        o_ps = [sem(f"o_ps{L}") for L in range(DEPTH)]
        x_ok = [sem(f"x_ok{L}") for L in range(DEPTH)]
        s_pads = sem("s_pads")
        bias_ok = sem("bias_ok")
        bias_used = sem("bias_used")
        qp_ok = sem("qp_ok")
        qf_ok = sem("qf_ok")
        sc_ps = [sem(f"sc_ps{i}") for i in range(2)]
        lat_ok = [sem(f"lat_ok{i}") for i in range(2)]
        nmx_ok = [sem(f"nmx_ok{i}") for i in range(2)]
        exp_ok = [sem(f"exp_ok{i}") for i in range(2)]
        pt_ps = [sem(f"pt_ps{i}") for i in range(2)]
        pt_act = [sem(f"pt_act{i}") for i in range(2)]
        pt_dve = [sem(f"pt_dve{i}") for i in range(2)]
        pv_ok = [sem(f"pv_ok{i}") for i in range(2)]
        at_chain = sem("at_chain")
        at_ok = sem("at_ok")
        atT_ps = sem("atT_ps")
        atT_ok = sem("atT_ok")
        u_in = [[sem(f"u_in{L}_{i}") for i in range(G)] for L in range(DEPTH)]
        v_in = [[sem(f"v_in{L}_{i}") for i in range(G)] for L in range(DEPTH)]
        u_free = [sem(f"u_free{L}") for L in range(DEPTH)]
        v_free = [sem(f"v_free{L}") for L in range(DEPTH)]
        gel_ok = [sem(f"gel_ok{L}") for L in range(DEPTH)]
        w_ok = [sem(f"w_ok{L}") for L in range(DEPTH)]
        dg_in = [sem(f"dg_in{L}") for L in range(DEPTH)]
        q_ps = [sem(f"q_ps{L}") for L in range(DEPTH)]
        q_ok = [sem(f"q_ok{L}") for L in range(DEPTH)]
        qT_ps = [sem(f"qT_ps{L}") for L in range(DEPTH)]
        qT_ok = [sem(f"qT_ok{L}") for L in range(DEPTH)]
        s_ps = [sem(f"s_ps{L}") for L in range(DEPTH)]
        s_read = [sem(f"s_read{L}") for L in range(DEPTH)]
        tk = [sem(f"tk{L}") for L in range(DEPTH)]
        idx_ok = [sem(f"idx_ok{L}") for L in range(DEPTH)]
        top_ok = [sem(f"top_ok{L}") for L in range(DEPTH)]
        gexp_ok = [sem(f"gexp_ok{L}") for L in range(DEPTH)]
        hn_chain = [sem(f"hn_chain{L}") for L in range(DEPTH)]
        hn_ok = [sem(f"hn_ok{L}") for L in range(DEPTH)]
        hT_ps = [sem(f"hT_ps{L}") for L in range(DEPTH)]
        hT_ok = [sem(f"hT_ok{L}") for L in range(DEPTH)]
        hc_ok = [sem(f"hc_ok{L}") for L in range(DEPTH)]
        y_ok = [sem(f"y_ok{L}") for L in range(DEPTH)]
        y_read = [sem(f"y_read{L}") for L in range(DEPTH)]
        fchain = [sem(f"fchain{L}") for L in range(DEPTH)]
        f_sq = sem("f_sq")
        f_var = sem("f_var")
        f_std = sem("f_std")
        f_out = sem("f_out")

        NITEM = NT * PH
        NGRP = 2 * NITEM
        NSMALL = 6
        CH_A = 4
        CH_MIX = [6, 2]
        CH_B = 2 * N_MOD - CH_A
        CH_ALL = [CH_A + CH_MIX[L] + CH_B + 2 for L in range(DEPTH)]

        block = ctx.enter_context(nc.Block())

        @block.sync
        def _(sp):
            sp.dma_start(ident[:], ident_in).then_inc(s_small, 16)
            sp.dma_start(craw[:], cT).then_inc(s_small, 16)
            sp.dma_start(norms[:], normT).then_inc(s_small, 16)
            sp.dma_start(bmod[:], bmodT).then_inc(s_small, 16)
            sp.dma_start(iota16[:], iota_in).then_inc(s_small, 16)
            sp.dma_start(keys[:], keysT).then_inc(s_small, 16)
            for t in range(NT):
                sp.dma_start(xres[:, t, :], x[t * P:(t + 1) * P, :]).then_inc(s_x, 16)
            for t in range(NC):
                sp.dma_start(xctx[:, t, :], ctx_in[t * P:(t + 1) * P, :]).then_inc(s_ctxin, 16)

            def chunk(L, c, src, k=KD):
                if c >= SLOTS:
                    sp.wait_ge(w_free[L], c - SLOTS + 1)
                sp.dma_start(ring[:, c % SLOTS, 0:k, :], src).then_inc(w_in[L][c % SLOTS], 16)

            def mod_src(L, c):
                return w_mod[L].rearrange("(k p) n -> p k n", p=P)[:, :, c * BIG:(c + 1) * BIG]

            def cols(w, c):
                return w.rearrange("(k p) n -> p k n", p=P)[:, :, c * BIG:(c + 1) * BIG]

            for L in range(DEPTH):
                if L:
                    sp.wait_ge(u_free[L - 1], (NGRP + 1) * G)
                    sp.wait_ge(v_free[L - 1], (NGRP + 1) * G)
                c = 0
                for i in range(CH_A):
                    chunk(L, c, mod_src(L, i))
                    c += 1
                if L == 0:
                    for first in (2, 4, 0):
                        for i in range(2):
                            chunk(L, c, cols(w_qkv, first + i))
                            c += 1
                else:
                    chunk(L, c, dft_ch.rearrange("(k p) n -> p k n", p=P), 2)
                    chunk(L, c + 1, dft_pos.rearrange("(k p) n -> p k n", p=P))
                    c += 2
                for i in range(CH_B):
                    chunk(L, c, mod_src(L, CH_A + i))
                    c += 1
                for i in range(2):
                    chunk(L, c, cols(w_o if L == 0 else w_fno, i))
                    c += 1
                assert c == CH_ALL[L]
                if L == 0:
                    sp.wait_ge(job[0], 12)
                    for v in range(3):
                        if v == 1:
                            sp.wait_ge(job[0], 48)
                            sp.dma_start(masks_sb, masks).then_inc(s_maskin, 16)
                        if v == 2:
                            sp.wait_ge(bias_used, 1)
                        for cc in range(COLS_T):
                            at = (PADC + SHIFT[v] - cc) * ROWS
                            sp.dma_start(bias[v][cc * ROWS:(cc + 1) * ROWS, :, :],
                                         bias_tab[:, :, at:at + WIN]).then_inc(s_bias[v], 16)
                sp.wait_ge(o_ps[L], 2 * NT)
                for c4 in range(4):
                    sp.dma_start(wq[:, :, c4 * BIG:(c4 + 1) * BIG], cols(w_query[L], c4)).then_inc(wq_in[L], 16)
            sp.wait_ge(hT_ps[1], NT)
            sp.wait_ge(hc_ok[1], NT)
            sp.dma_start(hx_next, norm_fin).then_inc(wfin_in, 16)
            for t in range(NT):
                sp.wait_ge(f_out, t + 1)
                sp.dma_start(out[t * P:(t + 1) * P, :], xres[:, t, :]).then_inc(s_out, 16)
            sp.wait_ge(s_out, 16 * NT)

        @block.gpsimd
        def _(pool):
            pool.memset(ones[:], 1.0).then_inc(s_ones, 1)
            pool.wait_ge(w_free[0], CH_ALL[0] - 2)
            for i in range(2):
                ins = pool.memset(p_mid[i], 0.0)
            ins.then_inc(s_pads, 1)
            pool.wait_ge(ev_dve[0], 28)
            pool.wait_ge(ev_act[0], 28)
            pool.wait_ge(s_maskin, 16)

            def add_mask(v):
                pool.wait_ge(s_bias[v], 16 * COLS_T)
                pool.tensor_tensor(bias[v], bias[v], masks_sb[:, v, :].unsqueeze(1).to_broadcast([P, HEADS, WIN]),
                                   ALU.add).then_inc(bias_ok, 1)

            add_mask(0)
            add_mask(1)
            for b in range(NT):
                if b == 2:
                    add_mask(2)

                def qcopy(j, nn):
                    pool.tensor_copy(qpair, qT[:, j, b * P:(b + 1) * P]).then_inc(qp_ok, 1)
                    hold(pool, qp_ok, nn + 1)
                    for hh in range(2):
                        ins = pool.tensor_scalar(qfix[hh], qpair, iota16[:, TOPK + hh:TOPK + hh + 1],
                                                 None, ALU.mult)
                    ins.then_inc(qf_ok, 1)

                if b:
                    pool.wait_ge(sc_ps[1], PAIRS * b)
                qcopy(0, PAIRS * b)
                with pool.Fori(1, PAIRS) as j:
                    hold(pool, sc_ps[1], j + PAIRS * b)
                    qcopy(j, j + PAIRS * b)

            for L in range(DEPTH):
                def gather(table, rows, b, g8, par, arrived):
                    pool.indirect_dma_start(out=rows[:, b, :], out_offset=None, in_=table,
                                            in_offset=bass.IndirectOffsetOnAxis(ap=idx[par][:, g8 + b:g8 + b + 1],
                                                                                axis=0)).then_inc(arrived[b], 16)

                def u_group(grp, off, par):
                    for b in range(G):
                        if b % 4 == 0:
                            hold(pool, u_free[L], G * grp + b + 4)
                        gather(peer_u[L], urows, b, off * G, par, u_in[L])

                def v_group(grp, off, par):
                    for b in range(G):
                        if b % 4 == 0:
                            hold(pool, v_free[L], G * grp + b + 4)
                        gather(peer_v[L], vrows, b, off * G, par, v_in[L])

                def pair(m, first):
                    for par in range(2):
                        hold(pool, idx_ok[L], 2 * m + par + 1)
                        u_group(4 * m + 2 * par, 0, par)
                        if not (first and par == 0):
                            v_group(4 * m + 2 * par - 1, 1, 1 - par)
                        u_group(4 * m + 2 * par + 1, 1, par)
                        v_group(4 * m + 2 * par, 0, par)

                pool.wait_ge(x_ok[L], NT)
                pool.wait_ge(sq_done[L], NT + (NC if L == 0 else 0) + NT)
                pair(0, True)
                with pool.Fori(1, NITEM // 2) as m:
                    pair(m, False)
                v_group(NGRP - 1, 1, 1)

        @block.tensor
        def _(pe):
            pe.wait_ge(s_small, 16 * NSMALL)
            pe.wait_ge(s_ones, 1)
            pe.wait_ge(s_silu, 1)
            for L in range(DEPTH):
                n = [0]

                def bank():
                    i = n[0]
                    if i >= 4:
                        pe.wait_ge((ev_dve if i % 2 == 0 else ev_act)[L], (i - 4) // 2 + 1)
                    return ps[:, i % 4, :]

                def done(ins):
                    ins.then_inc(job[L], 1)
                    n[0] += 1

                def chunk_wait(c):
                    pe.wait_ge(w_in[L][c % SLOTS], 16 * (c // SLOTS + 1))
                    return ring[:, c % SLOTS, :, :]

                def chunk_used():
                    pe.wait_ge(job[L], n[0])
                    pe.sem_inc(w_free[L], 1)

                def mod_chunk(c, i):
                    w = chunk_wait(c)
                    for blk in range(4):
                        j = 4 * i + blk
                        for k in range(KD):
                            ins = pe.matmul(ps[:, 7, 2 * j:2 * j + 2], w[:, k, blk * P:(blk + 1) * P],
                                            silu[:, k, :], start=(k == 0), stop=(k == KD - 1))
                    ins.then_inc(w_free[L], 1)

                if L:
                    pe.wait_ge(hT_ok[L - 1], 2 * NT)
                c = 0
                for i in range(CH_A):
                    mod_chunk(c, i)
                    c += 1
                pe.wait_ge(xn_ok[L], NT + (NC if L == 0 else 0))
                if L:
                    pe.wait_ge(y_ok[L - 1], NT + 1)
                    pe.wait_ge(qT_ok[L - 1], NITEM)
                for k in range(KD):
                    dst = bank()
                    for t in range(NT):
                        ins = pe.transpose(dst[:, t * P:(t + 1) * P], xn[:, t, k * P:(k + 1) * P], ident[:])
                    done(ins)
                if L == 0:
                    for k2 in range(KD // 2):
                        dst = bank()
                        for kk in range(2):
                            for t in range(NC):
                                k = 2 * k2 + kk
                                ins = pe.transpose(dst[:, (2 * kk + t) * P:(2 * kk + t + 1) * P],
                                                   xctx[:, t, k * P:(k + 1) * P], ident[:])
                        done(ins)
                    pe.wait_ge(ev_dve[L], n[0] // 2)
                    pe.wait_ge(ev_act[L], n[0] // 2)
                    for i in range(2):
                        w = chunk_wait(c)
                        for blk in range(4):
                            for src, width in ((hT, SEQ), (hcT, CTX)):
                                dst = bank()
                                for k in range(KD):
                                    ins = pe.matmul(dst[:, 0:width], w[:, k, blk * P:(blk + 1) * P], src[:, k, :],
                                                    start=(k == 0), stop=(k == KD - 1))
                                done(ins)
                        chunk_used()
                        c += 1
                    for i in range(2):
                        w = chunk_wait(c)
                        for t in range(NT + NC):
                            dst = bank()
                            for k in range(KD):
                                lhs = hT[:, k, t * P:(t + 1) * P] if t < NT else hcT[:, k, (t - NT) * P:(t - NT + 1) * P]
                                ins = pe.matmul(dst, lhs, w[:, k, :], start=(k == 0), stop=(k == KD - 1))
                            done(ins)
                        chunk_used()
                        c += 1
                    for i in range(2):
                        w = chunk_wait(c)
                        for blk in range(4):
                            dst = bank()
                            for k in range(KD):
                                ins = pe.matmul(dst, w[:, k, blk * P:(blk + 1) * P], hT[:, k, :],
                                                start=(k == 0), stop=(k == KD - 1))
                            done(ins)
                        chunk_used()
                        c += 1
                else:
                    pe.wait_ge(ev_dve[L], n[0] // 2)
                    pe.wait_ge(ev_act[L], n[0] // 2)
                    w = chunk_wait(c)
                    for t in range(NT):
                        for g in range(4):
                            dst = bank()
                            for kk in range(2):
                                ins = pe.matmul(dst, hT[:, 2 * g + kk, t * P:(t + 1) * P], w[:, kk, :],
                                                start=(kk == 0), stop=(kk == 1))
                            done(ins)
                    chunk_used()
                    c += 1
                    pe.wait_ge(ev_dve[L], n[0] // 2)
                    pe.wait_ge(ev_act[L], n[0] // 2)
                    w = chunk_wait(c)
                    for j in range(KD):
                        dst = bank()
                        for i in range(8):
                            part, t = i // NT, i % NT
                            at = part * 256 + (j % 2) * P
                            ins = pe.matmul(dst, cs[:, t, j // 2, at:at + P], w[:, i, :], start=(i == 0), stop=(i == 7))
                        done(ins)
                    chunk_used()
                    c += 1
                pe.wait_ge(mod_ok[L], 1)
                for i in range(CH_B):
                    mod_chunk(c, CH_A + i)
                    c += 1
                for v in range(4):
                    pe.wait_ge(dg_ok[L], v + 1)
                    for half in range(2):
                        dst = bank()
                        done(pe.matmul(dst, ones[:], modb[:, v, half * 512:(half + 1) * 512], start=True, stop=True))
                pe.wait_ge(ev_dve[L], n[0] // 2)
                pe.wait_ge(ev_act[L], n[0] // 2)

                wout = [chunk_wait(c), chunk_wait(c + 1)]

                def out_proj(t, lhs):
                    for half in range(2):
                        if t:
                            pe.wait_ge(x_ok[L], t)
                        for k in range(KD):
                            ins = pe.matmul(ps[:, 4 + half, :], lhs(k), wout[half][:, k, :],
                                            start=(k == 0), stop=(k == KD - 1))
                        ins.then_inc(o_ps[L], 1)

                if L == 0:
                    pe.wait_ge(s_pads, 1)
                    for b in range(NT):
                        def scores(j, hh, nn):
                            if hh == 0:
                                pe.wait_ge(qf_ok, nn + 1)
                            pe.matmul(ps[:, hh, 0:WIN], qfix[hh], kT[:, j, WSTART[b]:WSTART[b] + WIN],
                                      start=True, stop=True)
                            pe.matmul(ps[:, hh, WIN:WIN + CTX], qfix[hh], kcT[:, j, :],
                                      start=True, stop=True).then_inc(sc_ps[hh], 1)

                        def values(j, hh, nn):
                            if VARIANT[b] == 1:
                                prob, tiles = p_mid[hh], [b - 1, b, b + 1, NT, NT + 1]
                            else:
                                prob, tiles = p_edge[hh], [WSTART[b] // P, WSTART[b] // P + 1, NT, NT + 1]
                            pe.wait_ge(exp_ok[hh], nn + 1)
                            for i in range(4):
                                ins = pe.transpose(ps[:, 2 + hh, i * P:(i + 1) * P], prob[:, i * P:(i + 1) * P], ident[:])
                            if len(tiles) == 5:
                                ins = pe.transpose(ps[:, 4, hh * P:(hh + 1) * P], prob[:, 4 * P:5 * P], ident[:])
                            ins.then_inc(pt_ps[hh], 1)
                            pe.wait_ge(pt_act[hh], nn + 1)
                            if VARIANT[b] == 1:
                                pe.wait_ge(pt_dve[hh], nn - PAIRS + 1)
                            dst = ps[:, 6:8, :].rearrange("p a n -> p (a n)")
                            for i, tile in enumerate(tiles):
                                ins = pe.matmul(dst[:, bass.ds((2 * j + hh) * DH, DH)], pT[hh][:, i * P:(i + 1) * P],
                                                vtok[:, tile, bass.ds((2 * j + hh) * DH, DH)],
                                                start=(i == 0), stop=(i == len(tiles) - 1))
                            ins.then_inc(pv_ok[hh], 1)

                        base = b * PAIRS
                        if b:
                            pe.wait_ge(at_ok, b)
                            pe.wait_ge(x_ok[L], b)
                        scores(0, 0, base)
                        scores(0, 1, base)
                        with pe.Fori(0, PAIRS - 1) as j:
                            for hh in range(2):
                                values(j, hh, j + base)
                                scores(j + 1, hh, j + 1 + base)
                        for hh in range(2):
                            values(PAIRS - 1, hh, PAIRS - 1 + base)
                        pe.wait_ge(at_ok, b + 1)
                        for k in range(KD):
                            ins = pe.transpose(ps[:, 2 + k // 4, (k % 4) * P:(k % 4 + 1) * P],
                                               attn[:, k * P:(k + 1) * P], ident[:])
                        ins.then_inc(atT_ps, 1)
                        pe.wait_ge(atT_ok, b + 1)
                        out_proj(b, lambda k: attnT[:, k, :])
                else:
                    for t in range(NT):
                        out_proj(t, lambda k: fT[:, k, t * P:(t + 1) * P])

                def turn_h(nt):
                    pe.wait_ge(hn_ok[L], nt + 1)
                    for k in range(KD):
                        ins = pe.transpose(ps[:, 6 + k // 4, (k % 4) * P:(k % 4 + 1) * P],
                                           hx_next[:, k * P:(k + 1) * P], ident[:])
                    ins.then_inc(hT_ps[L], 1)

                def head_scores(head, i, par, first=False):
                    if not first:
                        pe.wait_ge(q_ok[L], i)
                    for k in range(KD):
                        ins = pe.matmul(ps[:, 2, 0:256], hxT[:, k, :], wq[:, k, bass.ds(head * 256, 256)],
                                        start=(k == 0), stop=(k == KD - 1))
                    ins.then_inc(q_ps[L], 1)
                    pe.wait_ge(q_ok[L], i + 1)
                    for a in range(2):
                        ins = pe.transpose(ps[:, 3, a * P:(a + 1) * P], q_sb[:, a * P:(a + 1) * P], ident[:])
                    ins.then_inc(qT_ps[L], 1)
                    pe.wait_ge(qT_ok[L], i + 1)
                    pe.wait_ge(s_read[L], i + 1)
                    for a in range(2):
                        ins = pe.matmul(ps[:, 4 + par, a * P:(a + 1) * P], qT_sb[:, a, :], keys[:, L, a, :],
                                        start=True, stop=True)
                    ins.then_inc(s_ps[L], 1)

                def add_rows(grp, start):
                    for b in range(G):
                        pe.wait_ge(dg_in[L], G * grp + b + 1)
                        pe.wait_ge(v_in[L][b], 16 * grp + 16)
                        for half in range(2):
                            ins = pe.matmul(ps[:, half, :], diag[:, b, :], vrows[:, b, half * 512:(half + 1) * 512],
                                            start=(start and b == 0), stop=False, skip_group_check=True)
                        ins.then_inc(v_free[L], 1)

                def pair(m, next_head, tile_start, chain=True):
                    for par in range(2):
                        add_rows(4 * m + 2 * par, tile_start and par == 0)
                        if chain:
                            head_scores(next_head + par, 2 * m + par + 2, par)
                        add_rows(4 * m + 2 * par + 1, False)

                def tile(t, last):
                    hold(pe, y_ok[L], t + 1)
                    pair(NPAIR_T * t, 2, True)
                    with pe.Fori(1, NPAIR_T - 1) as pr:
                        pair(NPAIR_T * t + pr, 2 * pr + 2, False)
                    if not last:
                        turn_h(t + 1)
                        hold(pe, hT_ok[L], 2 * t + 4)
                    pair(NPAIR_T * t + NPAIR_T - 1, 0, False, chain=not last)

                pe.wait_ge(x_ok[L], NT)
                if L == 0:
                    pe.wait_ge(at_ok, NT)
                pe.sem_inc(v_free[L], G)
                turn_h(0)
                pe.wait_ge(hT_ok[L], 2)
                pe.wait_ge(wq_in[L], 16 * 4)
                head_scores(0, 0, 0, first=True)
                head_scores(1, 1, 1)
                tile(0, False)
                with pe.Fori(1, NT - 1) as t:
                    tile(t, False)
                tile(NT - 1, True)

        @block.scalar
        def _(act):
            act.wait_ge(s_small, 16 * NSMALL)
            act.activation(silu[:], craw[:], ACT.Silu).then_inc(s_silu, 1)
            act.wait_ge(s_x, 16 * NT)
            act.wait_ge(s_ctxin, 16 * NC)
            nrm = 0
            for L in range(DEPTH):
                tiles = [xres[:, t, :] for t in range(NT)] + ([xctx[:, t, :] for t in range(NC)] if L == 0 else [])
                if L:
                    act.wait_ge(y_read[L - 1], NT + 1)
                for i, src in enumerate(tiles):
                    act.activation(xn[:, 0, :], src, ACT.Square,
                                   accum_out=ss[:, i:i + 1]).then_inc(sq_done[L], 1)
                    act.wait_ge(sq_done[L], i + 1)
                act.wait_ge(var_ok[L], 1)
                act.activation(rstd[:, 0:len(tiles)], ss[:, 0:len(tiles)], ACT.Sqrt).then_inc(std_ok[L], 1)
                act.wait_ge(rstd_ok[L], 1)
                for i, src in enumerate(tiles):
                    dst = xn[:, i, :] if i < NT else src
                    act.activation(dst, src, ACT.Copy, scale=rstd[:, i:i + 1]).then_inc(xn_ok[L], 1)

                def evac(i, outs, ins_, scales=None, shifts=None, scale=1.0):
                    if i % 2 == 0:
                        return
                    act.wait_ge(job[L], i + 1)
                    for q, (o, s) in enumerate(zip(outs, ins_)):
                        if scales is not None:
                            ins = act.activation(o, s, ACT.Identity, bias=shifts[q], scale=scales[q])
                        else:
                            ins = act.activation(o, s, ACT.Copy, scale=scale)
                    ins.then_inc(ev_act[L], 1)

                act.wait_ge(mod_ok[L], 1)
                dense_copies(L, evac, ps, modc, a_mix, hT, hcT, kT, kcT, vtok, qT, cs, fT, modb)

                if L == 0:
                    for b in range(NT):
                        def soft(hh, nn, h):
                            prob = p_edge[hh].rearrange("p (a n) -> p a n", a=2)
                            if VARIANT[b] == 1:
                                prob = p_mid[hh].rearrange("p (a n) -> p a n", a=2)[:, :, 64:64 + WIN]
                            act.wait_ge(nmx_ok[hh], nn + 1)
                            act.activation(prob, ps[:, hh, :].rearrange("p (a n) -> p a n", a=2), ACT.Exp,
                                           bias=nmx[:, hh:hh + 1], accum_out=esum[:, h]).then_inc(exp_ok[hh], 1)

                        def turned(hh, nn):
                            act.wait_ge(pt_ps[hh], nn + 1)
                            act.activation(pT[hh][:, 0:512], ps[:, 2 + hh, :], ACT.Copy).then_inc(pt_act[hh], 1)

                        base = b * PAIRS
                        for hh in range(2):
                            soft(hh, base, slice(hh, hh + 1))
                        with act.Fori(0, PAIRS - 1) as j:
                            for hh in range(2):
                                turned(hh, j + base)
                                soft(hh, j + 1 + base, bass.ds(2 * j + 2 + hh, 1))
                        for hh in range(2):
                            turned(hh, PAIRS - 1 + base)
                        act.wait_ge(atT_ps, b + 1)
                        act.activation(attnT, ps[:, 2:4, :].rearrange("p a (k n) -> p (a k) n", k=4),
                                       ACT.Copy).then_inc(atT_ok, 1)
                base_sq = len(tiles)
                for t in range(NT):
                    act.wait_ge(x_ok[L], t + 1)
                    act.wait_ge(sq_done[L], base_sq + t)
                    act.activation(sqj, xres[:, t, :], ACT.Square, accum_out=ss[:, t:t + 1]).then_inc(sq_done[L], 1)
                act.wait_ge(var_ok[L], 2)
                act.activation(rstd[:, 0:NT], ss[:, 0:NT], ACT.Sqrt).then_inc(std_ok[L], 1)

                def turned_h(nt):
                    act.wait_ge(hT_ps[L], nt + 1)
                    for a in range(2):
                        act.activation(hxT[:, 4 * a:4 * a + 4, :], ps[:, 6 + a, :].rearrange("p (k n) -> p k n", k=4),
                                       ACT.Copy).then_inc(hT_ok[L], 1)

                def query_copies(i):
                    act.wait_ge(q_ps[L], i + 1)
                    act.activation(q_sb, ps[:, 2, 0:256], ACT.Copy).then_inc(q_ok[L], 1)
                    act.wait_ge(qT_ps[L], i + 1)
                    act.activation(qT_sb, ps[:, 3, 0:256].rearrange("p (a n) -> p a n", a=2),
                                   ACT.Copy).then_inc(qT_ok[L], 1)

                def gate_exp(i, par):
                    act.wait_ge(top_ok[L], i + 1)
                    act.activation(gate_e[par][:], tops, ACT.Exp, bias=gneg[:],
                                   accum_out=gsum[:]).then_inc(gexp_ok[L], 1)

                def gelu(grp, gp):
                    act.wait_ge(u_free[L], G * grp + 2 * G)
                    act.activation(gel[:, gp, :], pre[:, gp, :], ACT.Gelu).then_inc(gel_ok[L], 1)

                def diags(grp, gp):
                    act.wait_ge(w_ok[L], grp + 1)
                    for b in range(G):
                        act.wait_ge(v_free[L], G * grp + b + 1)
                        act.activation(diag[:, b, :], ident[:], ACT.Copy,
                                       scale=wgt[:, gp, b:b + 1]).then_inc(dg_in[L], 1)

                def pair(m, chain=True, last=False):
                    for par in range(2):
                        g0 = 4 * m + 2 * par
                        gelu(g0, 0)
                        diags(g0, 0)
                        if chain:
                            query_copies(2 * m + par + 2)
                        gelu(g0 + 1, 1)
                        if not (last and par == 1):
                            gate_exp(2 * m + par + 1, 1 - par)
                        diags(g0 + 1, 1)

                def tile(t, last):
                    with act.Fori(0, NPAIR_T - 1) as pr:
                        pair(NPAIR_T * t + pr)
                    if not last:
                        turned_h(t + 1)
                    pair(NPAIR_T * t + NPAIR_T - 1, chain=not last, last=last)
                    act.wait_ge(v_free[L], G * 2 * PH * (t + 1) + G)
                    act.wait_ge(y_read[L], t + 1)
                    act.activation(ytmp, ps[:, 0:2, :].rearrange("p a n -> p (a n)"), ACT.Copy).then_inc(y_ok[L], 1)

                act.sem_inc(y_ok[L], 1)
                turned_h(0)
                query_copies(0)
                query_copies(1)
                gate_exp(0, 0)
                tile(0, False)
                with act.Fori(1, NT - 1) as t:
                    tile(t, False)
                tile(NT - 1, True)
            act.wait_ge(f_var, 1)
            act.activation(rstd[:, 0:NT], ss[:, 0:NT], ACT.Sqrt).then_inc(f_std, 1)

        @block.vector
        def _(dve):
            dve.wait_ge(s_small, 16 * NSMALL)
            for L in range(DEPTH):
                ch = Count(dve, dchain[L])
                nt_ln = NT + (NC if L == 0 else 0)

                def rms(num, k):
                    dve.tensor_scalar(ss[:, 0:num], ss[:, 0:num], 1.0 / D, EPS, ALU.mult, ALU.add).then_inc(var_ok[L], 1)
                    dve.wait_ge(std_ok[L], k)
                    dve.reciprocal(rstd[:, 0:num], rstd[:, 0:num]).then_inc(rstd_ok[L], 1)

                dve.wait_ge(sq_done[L], nt_ln)
                rms(nt_ln, 1)
                dve.wait_ge(w_free[L], CH_A)
                nA = 4 * CH_A
                ch.step(dve.tensor_tensor(modc[:, 0:nA, :], ps[:, 7, 0:2 * nA].rearrange("p (j n) -> p j n", n=2),
                                          bmod[:, L, 0:nA].unsqueeze(2).to_broadcast([P, nA, 2]), ALU.add))
                ch.step(dve.tensor_scalar(a_mix[:], modc[:, KD:2 * KD, :], 1.0, None, ALU.add))
                dve.tensor_tensor(a_mix[:], a_mix[:], norms[:, L, :].unsqueeze(2).to_broadcast([P, KD, 2]),
                                  ALU.mult).then_inc(mod_ok[L], 1)
                dve.wait_ge(mod_ok[L], 1)

                def evac(i, outs, ins_, scales=None, shifts=None, scale=1.0):
                    if i % 2:
                        return
                    dve.wait_ge(job[L], i + 1)
                    for q, (o, s) in enumerate(zip(outs, ins_)):
                        if scales is not None:
                            ins = dve.tensor_scalar(o, s, scales[q], shifts[q], ALU.mult, ALU.add)
                        elif scale != 1.0:
                            ins = dve.tensor_scalar(o, s, scale, None, ALU.mult)
                        else:
                            ins = dve.tensor_copy(o, s)
                    ins.then_inc(ev_dve[L], 1)

                def mod_b():
                    dve.wait_ge(w_free[L], CH_A + CH_MIX[L] + CH_B)
                    ch.step(dve.tensor_tensor(modc[:, nA:MODB, :],
                                              ps[:, 7, 2 * nA:2 * MODB].rearrange("p (j n) -> p j n", n=2),
                                              bmod[:, L, nA:MODB].unsqueeze(2).to_broadcast([P, MODB - nA, 2]), ALU.add))
                    ch.step(dve.tensor_scalar(a_ffn[:], modc[:, 4 * KD:5 * KD, 0], 1.0, None, ALU.add))
                    ch.step(dve.tensor_tensor(a_ffn[:], a_ffn[:], norms[:, DEPTH + L, :], ALU.mult))
                    for v, col in ((AF, a_ffn[:]), (SHF, modc[:, 3 * KD:4 * KD, 0]), (GF, modc[:, 5 * KD:6 * KD, 0]),
                                   (GM, modc[:, 2 * KD:3 * KD, 0])):
                        dve.tensor_tensor(modb[:, v, :].rearrange("p (k n) -> p k n", k=KD),
                                          ident[:, :].unsqueeze(1).to_broadcast([P, KD, P]),
                                          col.unsqueeze(2).to_broadcast([P, KD, P]), ALU.mult).then_inc(dg_ok[L], 1)

                jobs = dense_copies(L, evac, ps, modc, a_mix, hT, hcT, kT, kcT, vtok, qT, cs, fT, modb, mod_b)
                dve.wait_ge(ev_act[L], jobs // 2)

                def residual(t):
                    dve.wait_ge(o_ps[L], 2 * t + 2)
                    ch.step(dve.tensor_tensor(otmp, ps[:, 4:6, :].rearrange("p a n -> p (a n)"), modb[:, GM, :], ALU.mult))
                    dve.tensor_tensor(xres[:, t, :], xres[:, t, :], otmp, ALU.add).then_inc(x_ok[L], 1)
                    dve.wait_ge(x_ok[L], t + 1)

                if L == 0:
                    for b in range(NT):
                        def masked(hh, nn, h):
                            hold(dve, sc_ps[hh], nn + 1)
                            dve.tensor_tensor(ps[:, hh, 0:WIN], ps[:, hh, 0:WIN], bias[VARIANT[b]][:, h, :],
                                              ALU.add).then_inc(lat_ok[hh], 1)
                            hold(dve, lat_ok[hh], nn + 1)
                            dve.tensor_reduce(nmx[:, hh:hh + 1], ps[:, hh, :], AX.X, ALU.max,
                                              negate=True).then_inc(nmx_ok[hh], 1)

                        def turned(hh, nn):
                            if VARIANT[b] == 1:
                                hold(dve, pt_ps[hh], nn + 1)
                                dve.tensor_copy(pT[hh][:, 512:640], ps[:, 4, hh * P:(hh + 1) * P]).then_inc(pt_dve[hh], 1)

                        base = b * PAIRS
                        dve.wait_ge(bias_ok, (2, 2, 3)[VARIANT[b]])
                        for hh in range(2):
                            masked(hh, base, slice(hh, hh + 1))
                        with dve.Fori(0, PAIRS - 1) as j:
                            for hh in range(2):
                                turned(hh, j + base)
                                masked(hh, j + 1 + base, bass.ds(2 * j + 2 + hh, 1))
                        for hh in range(2):
                            turned(hh, PAIRS - 1 + base)
                        dve.wait_ge(exp_ok[1], (b + 1) * PAIRS)
                        ch.step(dve.reciprocal(einv[:], esum[:]))
                        dve.sem_inc(bias_used, 1)
                        dve.wait_ge(pv_ok[1], (b + 1) * PAIRS)
                        dve.tensor_tensor(attn.rearrange("p (h n) -> p h n", h=HEADS),
                                          ps[:, 6:8, :].rearrange("p a (h n) -> p (a h) n", h=PAIRS),
                                          einv[:].unsqueeze(2).to_broadcast([P, HEADS, DH]), ALU.mult).then_inc(at_ok, 1)
                        residual(b)
                else:
                    for t in range(NT):
                        residual(t)
                dve.wait_ge(sq_done[L], nt_ln + NT)
                rms(NT, 2)
                dve.wait_ge(rstd_ok[L], 2)

                def prep(t, col):
                    dve.scalar_tensor_tensor(hx_next, xres[:, t, :], rstd[:, col], modb[:, AF, :],
                                             ALU.mult, ALU.mult).then_inc(hn_chain[L], 1)
                    hold(dve, hn_chain[L], t + 1)
                    dve.tensor_tensor(hx_next, hx_next, modb[:, SHF, :], ALU.add).then_inc(hn_ok[L], 1)

                def take_h(t):
                    hold(dve, hn_ok[L], t + 1)
                    hold(dve, u_free[L], 2 * PH * G * t + G)
                    dve.tensor_copy(hx_cur, hx_next).then_inc(hc_ok[L], 1)
                    hold(dve, hc_ok[L], t + 1)

                def dots(grp, gp):
                    for b in range(G):
                        dve.wait_ge(u_in[L][b], 16 * grp + 16)
                        dve.tensor_tensor_reduce(urows[:, b, :], urows[:, b, :], hx_cur, 1.0, 0.0, ALU.mult, ALU.add,
                                                 pre[:, gp, b:b + 1]).then_inc(u_free[L], 1)

                def weights(grp, gp, par):
                    hold(dve, gel_ok[L], grp + 1)
                    dve.scalar_tensor_tensor(wgt[:, gp, :], gel[:, gp, :], gate_r[par][:],
                                             gate_e[par][:, gp * G:(gp + 1) * G],
                                             ALU.mult, ALU.mult).then_inc(w_ok[L], 1)

                def halves(i, par):
                    ct = Count(dve, tk[L], KSTEPS * i)
                    score = [ps[:, 4 + par, a * P:(a + 1) * P] for a in range(2)]
                    hold(dve, s_ps[L], i + 1)
                    dve.max(topv[:, 0, 0:8], score[0])
                    ct.step(dve.max(topv[:, 1, 0:8], score[1]))
                    for a in range(2):
                        dve.match_replace(wk[:, a, :], topv[:, a, 0:8], score[a], NEG)
                    dve.max_index(ixu[:, 0, 0:8], topv[:, 0, 0:8], score[0])
                    dve.max_index(ixu[:, 1, 0:8], topv[:, 1, 0:8], score[1]).then_inc(s_read[L], 1)
                    hold(dve, s_read[L], i + 3)
                    dve.max(topv[:, 0, 8:16], wk[:, 0, :])
                    ct.step(dve.max(topv[:, 1, 8:16], wk[:, 1, :]))
                    dve.max_index(ixu[:, 0, 8:16], topv[:, 0, 8:16], wk[:, 0, :])
                    ct.step(dve.max_index(ixu[:, 1, 8:16], topv[:, 1, 8:16], wk[:, 1, :]))
                    dve.tensor_tensor(cand.rearrange("p (a b) -> p a b", a=TOPK),
                                      topv[:, 0, :].unsqueeze(2).to_broadcast([P, TOPK, TOPK]),
                                      topv[:, 1, :].unsqueeze(1).to_broadcast([P, TOPK, TOPK]), ALU.add)
                    dve.tensor_scalar(tab[:, 0, :], ixu[:, 0, :], float(NKEY), None, ALU.mult)
                    ct.step(dve.tensor_copy(tab[:, 1, :], ixu[:, 1, :]))
                    return ct

                def choose(i, par, ct):
                    ct.step(dve.max(tops[:, 0:8], cand))
                    dve.match_replace(cand2, tops[:, 0:8], cand, NEG)
                    ct.step(dve.max_index(pos[:, 0:8], tops[:, 0:8], cand))
                    dve.tensor_scalar(gneg[:], tops[:, 0:1], -1.0, None, ALU.mult)
                    dve.max(tops[:, 8:16], cand2).then_inc(top_ok[L], 1)
                    hold(dve, top_ok[L], i + 1)
                    ct.step(dve.max_index(pos[:, 8:16], tops[:, 8:16], cand2))
                    dve.tensor_scalar(poshl[:, :, 0], pos[:], 4, None, ALU.logical_shift_right)
                    ct.step(dve.tensor_scalar(poshl[:, :, 1], pos[:], TOPK - 1, None, ALU.bitwise_and))
                    oh = onehot.rearrange("p (k a n) -> p k a n", k=TOPK, a=2)
                    ct.step(dve.tensor_tensor(oh, poshl[:, :, :].unsqueeze(3).to_broadcast([P, TOPK, 2, TOPK]),
                                              iota16[:, 0:TOPK].unsqueeze(1).unsqueeze(1).to_broadcast([P, TOPK, 2, TOPK]),
                                              ALU.is_equal))
                    ct.step(dve.tensor_tensor(oh, oh, tab.unsqueeze(1).to_broadcast([P, TOPK, 2, TOPK]), ALU.mult))
                    if not isinstance(i, int) or i > 0:
                        hold(dve, v_free[L], 2 * G * i - G)
                    ct.step(dve.tensor_reduce(expert[:], onehot.rearrange("p (k n) -> p k n", k=TOPK), AX.X, ALU.add))
                    dve.tensor_copy(idx[par][:], expert[:]).then_inc(idx_ok[L], 1)
                    hold(dve, gexp_ok[L], i + 1)
                    ct.step(dve.reciprocal(gate_r[par][:], gsum[:]))
                    assert ct.n == KSTEPS, ct.n

                def pair(m, last=False):
                    for par in range(2):
                        i = 2 * m + par
                        more = not (last and par == 1)
                        dots(2 * i, 0)
                        if more:
                            ct = halves(i + 1, 1 - par)
                        weights(2 * i, 0, par)
                        dots(2 * i + 1, 1)
                        if more:
                            choose(i + 1, 1 - par, ct)
                        weights(2 * i + 1, 1, par)

                def finish(t):
                    hold(dve, y_ok[L], t + 2)
                    dve.tensor_tensor(ytmp, ytmp, modb[:, GF, :], ALU.mult).then_inc(fchain[L], 1)
                    hold(dve, fchain[L], t + 1)
                    dve.tensor_tensor(xres[:, t, :], xres[:, t, :], ytmp, ALU.add).then_inc(y_read[L], 1)

                def tile(t, first, last):
                    with dve.Fori(0, NPAIR_T - 1) as pr:
                        pair(NPAIR_T * t + pr)
                    if not last:
                        hold(dve, hT_ps[L], t + 1)
                        prep(t + 1, slice(t + 1, t + 2) if isinstance(t, int) else bass.ds(t + 1, 1))
                    if not first:
                        finish(t - 1)
                    pair(NPAIR_T * t + NPAIR_T - 1, last)
                    if not last:
                        take_h(t + 1)

                dve.sem_inc(u_free[L], G)
                dve.sem_inc(s_read[L], 2)
                dve.sem_inc(y_read[L], 1)
                prep(0, slice(0, 1))
                take_h(0)
                choose(0, 0, halves(0, 0))
                tile(0, True, False)
                with dve.Fori(1, NT - 1) as t:
                    tile(t, False, False)
                tile(NT - 1, False, True)
                finish(NT - 1)
                dve.wait_ge(y_read[L], NT + 1)

            for t in range(NT):
                dve.tensor_tensor_reduce(vrows[:, t, :], xres[:, t, :], xres[:, t, :], 1.0, 0.0, ALU.mult, ALU.add,
                                         ss[:, t:t + 1]).then_inc(f_sq, 1)
            dve.wait_ge(f_sq, NT)
            dve.tensor_scalar(ss[:, 0:NT], ss[:, 0:NT], 1.0 / D, EPS, ALU.mult, ALU.add).then_inc(f_var, 1)
            dve.wait_ge(f_std, 1)
            dve.reciprocal(rstd[:, 0:NT], rstd[:, 0:NT]).then_inc(f_sq, 1)
            dve.wait_ge(f_sq, NT + 1)
            dve.wait_ge(wfin_in, 16)
            for t in range(NT):
                dve.scalar_tensor_tensor(xres[:, t, :], xres[:, t, :], rstd[:, t:t + 1], hx_next, ALU.mult,
                                         ALU.mult).then_inc(f_out, 1)


def dense_copies(L, evac, ps, modc, a_mix, hT, hcT, kT, kcT, vtok, qT, cs, fT, modb, mod_b=None):
    n = 0

    def bank():
        return ps[:, n % 4, :]

    for k in range(KD):
        evac(n, [hT[:, k, :]], [bank()], [a_mix[:, k, 0:1]], [modc[:, k, 0:1]])
        n += 1
    if L == 0:
        for k2 in range(KD // 2):
            evac(n, [hcT[:, 2 * k2 + i, :] for i in range(2)], [bank()[:, i * CTX:(i + 1) * CTX] for i in range(2)],
                 [a_mix[:, 2 * k2 + i, 1:2] for i in range(2)], [modc[:, 2 * k2 + i, 1:2] for i in range(2)])
            n += 1
        for m in range(KD):
            evac(n, [kT[:, m, :]], [bank()])
            n += 1
            evac(n, [kcT[:, m, :]], [bank()[:, 0:CTX]])
            n += 1
        for half in range(2):
            for t in range(NT + NC):
                evac(n, [vtok[:, t, half * BIG:(half + 1) * BIG]], [bank()])
                n += 1
        for m in range(KD):
            evac(n, [qT[:, m, :]], [bank()], scale=DH ** -0.5)
            n += 1
    else:
        for t in range(NT):
            for g in range(4):
                evac(n, [cs[:, t, g, :]], [bank()])
                n += 1
        for j in range(KD):
            evac(n, [fT[:, j, :]], [bank()])
            n += 1
    if mod_b is not None:
        mod_b()
    for v in range(4):
        for half in range(2):
            evac(n, [modb[:, v, half * BIG:(half + 1) * BIG]], [bank()])
            n += 1
    return n


def _window_masks():
    out = np.zeros((3, P, WIN), np.float32)
    for v, b in ((0, 0), (1, 1), (2, NT - 1)):
        q = b * COLS_T + np.arange(P) // ROWS
        k = (WSTART[b] + np.arange(WIN)) // ROWS
        start = np.clip(q - WIN_C // 2, 0, GRID_W - WIN_C)[:, None]
        out[v] = np.where((k[None] >= start) & (k[None] < start + WIN_C), 0.0, -1e30)
    return out


def _dft_tables():
    gd = D // 4
    a = 2 * np.pi * (np.outer(np.arange(gd), np.arange(gd)) % gd) / gd
    ch = np.concatenate([np.cos(a), np.sin(a)], 1) / np.sqrt(gd)
    tok = np.arange(SEQ)
    p = (tok % ROWS) * GRID_W + tok // ROWS
    b = 2 * np.pi * (np.outer(p, p) % SEQ) / SEQ
    pos = np.concatenate([np.cos(b), -np.sin(b)], 0) / np.sqrt(SEQ)
    return ch.astype(np.float32), pos.astype(np.float32)


def kernel(x, c, ctx, c_ctx, norm_mix, norm_ffn, w_mod, b_mod, na_w_qkv, na_w_o, na_rpb,
           fno_w_out, peer_w_query, peer_sub_keys, peer_u, peer_v, norm_final):
    import concourse.bacc as _bacc
    from concourse.bass_utils import run_bass_kernel_spmd as _run

    def blocks(v):
        v = np.asarray(v)
        v = v.reshape(v.shape[:-1] + (-1, P))
        return np.moveaxis(v, -1, 0)

    grid = np.asarray(x).reshape(ROWS, GRID_W, D).transpose(1, 0, 2).reshape(SEQ, D)
    cond = np.stack([np.asarray(c).reshape(D), np.asarray(c_ctx)], 0)
    rpb = np.asarray(na_rpb)[0]
    table = np.zeros((ROWS, HEADS, LENC, ROWS), np.float32)
    for r in range(ROWS):
        first = rpb.shape[1] // 2 - r
        table[r, :, PADC:PADC + rpb.shape[2], :] = rpb[:, first:first + ROWS, :].transpose(0, 2, 1)
    ch, pos = _dft_tables()
    u, v = np.asarray(peer_u), np.asarray(peer_v)
    arrays = {
        "x": grid, "cT": blocks(cond).transpose(0, 2, 1), "ctx_in": np.asarray(ctx)[0],
        "normT": blocks(np.concatenate([np.asarray(norm_mix), np.asarray(norm_ffn)], 0)),
        "w_mod": w_mod, "bmodT": blocks(b_mod), "w_qkv": np.asarray(na_w_qkv)[0], "w_o": np.asarray(na_w_o)[0],
        "bias_tab": table.reshape(ROWS, HEADS, LENC * ROWS), "masks": _window_masks().transpose(1, 0, 2),
        "w_fno": np.asarray(fno_w_out)[0], "w_query": peer_w_query,
        "keysT": np.asarray(peer_sub_keys).transpose(3, 0, 1, 2),
        "peer_u0": u[0], "peer_u1": u[1], "peer_v0": v[0], "peer_v1": v[1],
        "norm_fin": np.broadcast_to(np.asarray(norm_final), (P, D)),
        "dft_ch": ch, "dft_pos": pos, "ident_in": np.eye(P, dtype=np.float32),
        "iota_in": np.concatenate([np.broadcast_to(np.arange(TOPK), (P, TOPK)),
                                   np.repeat(np.eye(2), DH, 0)], 1).astype(np.float32),
    }
    nc = _bacc.Bacc("TRN2", target_bir_lowering=False, num_devices=1)
    args = {}
    for name in list(arrays):
        arrays[name] = np.ascontiguousarray(arrays[name])
        args[name] = nc.dram_tensor(name, arrays[name].shape, mybir.dt.from_np(arrays[name].dtype),
                                    kind="ExternalInput").ap()
    out = nc.dram_tensor("out", (SEQ, D), F32, kind="ExternalOutput").ap()
    build(nc, out=out, **args)
    r = _run(nc, [arrays], core_ids=[0])
    got = np.asarray(r.results[0]["out"])
    return np.ascontiguousarray(got.reshape(GRID_W, ROWS, D).transpose(1, 0, 2)).reshape(1, SEQ, D)
```

```python
from contextlib import ExitStack

import numpy as np
import concourse.bass as bass
from concourse import mybir

ALU = mybir.AluOpType
ACT = mybir.ActivationFunctionType
AX = mybir.AxisListType
F32 = mybir.dt.float32
U32 = mybir.dt.uint32

P = 128
D = 1024
KD = D // P
SEQ = 512
NT = SEQ // P
CTX = 256
NC = CTX // P
GRID_W = 64
ROWS = SEQ // GRID_W
HEADS = 16
PAIRS = HEADS // 2
DH = D // HEADS
WIN_C = 16
COLS_T = P // ROWS
WIN = 256
DEPTH = 2
N_MOD = 6
MODB = N_MOD * KD
PH = 8
NKEY = 128
TOPK = 16
G = 8
NPAIR_T = PH // 2
KSTEPS = 12
EPS = 1e-6
NEG = -3.0e38
BIG = 512
SLOTS = 4
WSTART = [min(max(P * b - WIN // 4, 0), SEQ - WIN) for b in range(NT)]
VARIANT = [0, 1, 1, 2]


def hold(eng, sem, value):
    eng.wait_ge(sem, value)
    eng.nop(nofuse=True)


class Count:

    def __init__(self, eng, sem, base=0):
        self.eng, self.sem, self.base, self.n = eng, sem, base, 0

    def sig(self, ins):
        self.n += 1
        ins.then_inc(self.sem, 1)

    def wait(self):
        if isinstance(self.base, int):
            self.eng.wait_ge(self.sem, self.base + self.n)
        else:
            hold(self.eng, self.sem, self.base + self.n)

    def step(self, ins):
        self.sig(ins)
        self.wait()


def build(nc, x, cT, ctx_in, normT, w_mod, bmodT, w_qkv, w_o, bias_in, w_fno, w_query, keysT,
          peer_u0, peer_u1, peer_v0, peer_v1, norm_fin, dft_ch, dft_pos, ident_in, iota_in, out):
    peer_u, peer_v = [peer_u0, peer_u1], [peer_v0, peer_v1]
    with ExitStack() as ctx:
        def sb(name, shape, dt=F32):
            return ctx.enter_context(nc.sbuf_tensor(name, shape, dt))

        def sem(name):
            return ctx.enter_context(nc.semaphore(name))

        r1 = sb("r1", [P, 16384])
        r2 = sb("r2", [P, 16384])
        r3 = sb("r3", [P, 6144])
        r5 = sb("r5", [P, 4096])
        xres = sb("xres", [P, NT, D])
        modb = sb("modb", [P, 4, D])
        AF, SHF, GF, GM = range(4)

        ring = r1[:, :].rearrange("p (s k n) -> p s k n", s=SLOTS, k=KD)
        urows = r1[:, 0:G * D].rearrange("p (g d) -> p g d", g=G)
        vrows = r1[:, G * D:2 * G * D].rearrange("p (g d) -> p g d", g=G)
        scratch = r1[:, 8192:16384]
        qfix = [scratch[:, 0:128], scratch[:, 128:256]]
        p_mid = [scratch[:, 256 + 640 * i:256 + 640 * (i + 1)] for i in range(2)]
        p_edge = [scratch[:, 1536 + 512 * i:1536 + 512 * (i + 1)] for i in range(2)]
        pT = [scratch[:, 2560 + 640 * i:2560 + 640 * (i + 1)] for i in range(2)]
        qpair = scratch[:, 3840:3968]
        attn = scratch[:, 4096:5120]
        attnT = scratch[:, 5120:6144].rearrange("p (k n) -> p k n", k=KD)
        otmp = scratch[:, 6144:7168]
        sqj = scratch[:, 7168:8192]
        macc = [modb[:, 0, 512 * i:512 * (i + 1)] for i in range(2)]
        arow = [modb[0:2, 1, 512 * i:512 * (i + 1)] for i in range(2)]
        hT = r2[:, 0:4096].rearrange("p (k n) -> p k n", k=KD)
        hcT = r2[:, 4096:6144].rearrange("p (k n) -> p k n", k=KD)
        qT = r2[:, 6144:10240].rearrange("p (k n) -> p k n", k=KD)
        kT = r2[:, 10240:14336].rearrange("p (k n) -> p k n", k=KD)
        kcT = r2[:, 14336:16384].rearrange("p (k n) -> p k n", k=KD)
        vtok = r3[:, :].rearrange("p (t n) -> p t n", t=NT + NC)
        xctx = vtok[:, NT:NT + NC, :]
        xn = r5[:, :].rearrange("p (t n) -> p t n", t=NT)
        bias_a = r5[:, :].rearrange("p (h n) -> p h n", h=HEADS)
        bias_b = r2[:, 0:4096].rearrange("p (h n) -> p h n", h=HEADS)
        bias = [bias_a, bias_b, bias_a]
        cs = r2[:, 4096:12288].rearrange("p (t g n) -> p t g n", t=NT, g=4)
        fT = r2[:, 12288:16384].rearrange("p (k n) -> p k n", k=KD)
        xn1 = r2[:, 12288:16384].rearrange("p (t n) -> p t n", t=NT)
        dft_sb = [r1[:, 0:1024].rearrange("p (k n) -> p k n", k=2), r1[:, 4096:8192].rearrange("p (k n) -> p k n", k=KD)]
        wq = r2[:, :].rearrange("p (c k n) -> p c k n", c=4, k=KD)
        hx_next, hx_cur = r5[:, 0:1024], r5[:, 1024:2048]
        hxT = r5[:, 2048:3072].rearrange("p (k n) -> p k n", k=KD)
        ytmp = r5[:, 3072:4096]
        otmps, sqjs = [otmp, ytmp], [sqj, r3[:, 3072:4096]]
        diag = r3[:, 0:1024].rearrange("p (g n) -> p g n", g=G)
        q_sb = r3[:, 1024:1280]
        qT_sb = r3[:, 1280:1536].rearrange("p (a n) -> p a n", a=2)
        wk = r3[:, 1536:1792].rearrange("p (a n) -> p a n", a=2)
        cand = r3[:, 1792:2048]
        cand2 = r3[:, 2048:2304]
        onehot = r3[:, 2304:2816]
        topv = r3[:, 2816:2848].rearrange("p (a n) -> p a n", a=2)
        tab = r3[:, 2848:2880].rearrange("p (a n) -> p a n", a=2)
        tops = r3[:, 2880:2896]

        ident = sb("ident", [P, P])
        ones = sb("ones", [P, P])
        iota16 = sb("iota16", [P, TOPK + 2])
        keys = sb("keys", [P, DEPTH, 2, NKEY])
        craw = sb("craw", [P, KD, 2])
        silu = sb("silu", [P, KD, 2])
        norms = sb("norms", [P, 2 * DEPTH, KD])
        bmod = sb("bmod", [P, DEPTH, MODB])
        modc = [sb(f"modc{L}", [P, MODB, 2 - L]) for L in range(DEPTH)]
        a_mix = [sb(f"a_mix{L}", [P, KD, 2 - L]) for L in range(DEPTH)]
        a_ffn = [sb(f"a_ffn{L}", [P, KD]) for L in range(DEPTH)]
        ss = sb("ss", [P, NT + NC])
        rstd = sb("rstd", [P, NT + NC])
        nmx = sb("nmx", [P, 2])
        esum = sb("esum", [P, HEADS])
        einv = sb("einv", [P, HEADS])
        ixu = sb("ixu", [P, 2, TOPK], U32)
        pos = sb("pos", [P, TOPK], U32)
        poshl = sb("poshl", [P, TOPK, 2], U32)
        idx = [sb(f"idx{i}", [P, TOPK], U32) for i in range(2)]
        gate_e = [sb(f"gate_e{i}", [P, TOPK]) for i in range(2)]
        gate_r = [sb(f"gate_r{i}", [P, 1]) for i in range(2)]
        expert = sb("expert", [P, TOPK])
        gsum = sb("gsum", [P, 1])
        gneg = sb("gneg", [P, 1])
        pre = sb("pre", [P, 2, G])
        gel = sb("gel", [P, 2, G])
        wgt = sb("wgt", [P, 2, G])
        ps = ctx.enter_context(nc.psum_tensor("ps", [P, 8, 512], F32))

        s_small = sem("s_small")
        s_x = sem("s_x")
        s_ctxin = sem("s_ctxin")
        s_bias = [sem(f"s_bias{v}") for v in range(3)]
        s_out = sem("s_out")
        wa_in = [sem(f"wa_in{i}") for i in range(4)]
        wp_in = [sem(f"wp_in{i}") for i in range(2)]
        wm_in = [sem(f"wm_in{i}") for i in range(2)]
        wf_in = [sem(f"wf_in{i}") for i in range(4)]
        wq_in = [[sem(f"wq_in{L}_{i}") for i in range(4)] for L in range(DEPTH)]
        wfin_in = sem("wfin_in")
        s_ones = sem("s_ones")
        s_silu = sem("s_silu")
        sq_done = [sem(f"sq_done{L}") for L in range(DEPTH + 1)]
        var_ok = [sem(f"var_ok{L}") for L in range(DEPTH + 1)]
        std_ok = [sem(f"std_ok{L}") for L in range(DEPTH + 1)]
        rstd_ok = [sem(f"rstd_ok{L}") for L in range(DEPTH + 1)]
        xn_ok = [sem(f"xn_ok{L}") for L in range(DEPTH)]
        a_ps = sem("a_ps")
        arow_ok = sem("arow_ok")
        acol_ps = sem("acol_ps")
        macc_c = sem("macc_c")
        macc_ok = sem("macc_ok")
        mcol_ps = sem("mcol_ps")
        mod_ok = [sem(f"mod_ok{L}") for L in range(DEPTH)]
        dg_ok = [sem(f"dg_ok{L}") for L in range(DEPTH)]
        job = [sem(f"job{L}") for L in range(DEPTH)]
        ev_act = [sem(f"ev_act{L}") for L in range(DEPTH)]
        ev_dve = [sem(f"ev_dve{L}") for L in range(DEPTH)]
        dchain = [sem(f"dchain{L}") for L in range(DEPTH)]
        o_ps = [sem(f"o_ps{L}") for L in range(DEPTH)]
        x_ok = [sem(f"x_ok{L}") for L in range(DEPTH)]
        s_pads = sem("s_pads")
        bias_used = sem("bias_used")
        qp_ok = sem("qp_ok")
        qf_ok = [sem(f"qf_ok{i}") for i in range(2)]
        sc_ps = [sem(f"sc_ps{i}") for i in range(2)]
        lat_ok = [sem(f"lat_ok{i}") for i in range(2)]
        nmx_ok = [sem(f"nmx_ok{i}") for i in range(2)]
        exp_ok = [sem(f"exp_ok{i}") for i in range(2)]
        pt_ps = [sem(f"pt_ps{i}") for i in range(2)]
        pt_act = [sem(f"pt_act{i}") for i in range(2)]
        pt_dve = [sem(f"pt_dve{i}") for i in range(2)]
        pv_ok = [sem(f"pv_ok{i}") for i in range(2)]
        at_chain = sem("at_chain")
        at_ok = sem("at_ok")
        atT_ps = sem("atT_ps")
        atT_ok = sem("atT_ok")
        u_in = [sem(f"u_in{i}") for i in range(G)]
        v_in = [sem(f"v_in{i}") for i in range(G)]
        u_free = [sem(f"u_free{L}") for L in range(DEPTH)]
        v_free = [sem(f"v_free{L}") for L in range(DEPTH)]
        gel_ok = [sem(f"gel_ok{L}") for L in range(DEPTH)]
        w_ok = [sem(f"w_ok{L}") for L in range(DEPTH)]
        dg_in = [sem(f"dg_in{L}") for L in range(DEPTH)]
        q_ps = [sem(f"q_ps{L}") for L in range(DEPTH)]
        q_ok = [sem(f"q_ok{L}") for L in range(DEPTH)]
        qT_ps = [sem(f"qT_ps{L}") for L in range(DEPTH)]
        qT_ok = [sem(f"qT_ok{L}") for L in range(DEPTH)]
        s_ps = [sem(f"s_ps{L}") for L in range(DEPTH)]
        s_read = [sem(f"s_read{L}") for L in range(DEPTH)]
        tk = [sem(f"tk{L}") for L in range(DEPTH)]
        idx_ok = [sem(f"idx_ok{L}") for L in range(DEPTH)]
        top_ok = [sem(f"top_ok{L}") for L in range(DEPTH)]
        gexp_ok = [sem(f"gexp_ok{L}") for L in range(DEPTH)]
        hn_chain = [sem(f"hn_chain{L}") for L in range(DEPTH)]
        hn_ok = [sem(f"hn_ok{L}") for L in range(DEPTH)]
        hT_ps = [sem(f"hT_ps{L}") for L in range(DEPTH)]
        hT_ok = [sem(f"hT_ok{L}") for L in range(DEPTH)]
        hc_ok = [sem(f"hc_ok{L}") for L in range(DEPTH)]
        y_ok = [sem(f"y_ok{L}") for L in range(DEPTH)]
        y_read = [sem(f"y_read{L}") for L in range(DEPTH)]
        fchain = [sem(f"fchain{L}") for L in range(DEPTH)]
        f_out = sem("f_out")

        NITEM = NT * PH
        NGRP = 2 * NITEM
        NSMALL = 6
        CH_A = 4
        NMACC = DEPTH * 2 * N_MOD - CH_A
        JOB_H, JOB_K, JOB_V, JOB_Q = 12, 16, 2 * (NT + NC), 8
        sums_after, m = {}, 0
        for i in range(JOB_H, JOB_H + JOB_K + JOB_V + JOB_Q, 2):
            num = 2 if i >= JOB_H + JOB_K and i % 4 == 0 else 1
            sums_after[i] = list(range(m, min(m + num, NMACC)))
            m += num
        assert m >= NMACC
        USED = [20, 28, 34, 40, 44, 48]
        OUT_BANK = [[4, 4, 4, 0], [0, 4, 0, 6]]

        block = ctx.enter_context(nc.Block())

        @block.sync
        def _(sp):
            sp.dma_start(ident[:], ident_in).then_inc(s_small, 16)
            sp.dma_start(craw[:], cT).then_inc(s_small, 16)
            sp.dma_start(norms[:], normT).then_inc(s_small, 16)
            sp.dma_start(bmod[:], bmodT).then_inc(s_small, 16)
            sp.dma_start(iota16[:], iota_in).then_inc(s_small, 16)
            sp.dma_start(keys[:], keysT).then_inc(s_small, 16)
            for t in range(NT):
                sp.dma_start(xres[:, t, :], x[t * P:(t + 1) * P, :]).then_inc(s_x, 16)
            for t in range(NC):
                sp.dma_start(xctx[:, t, :], ctx_in[t * P:(t + 1) * P, :]).then_inc(s_ctxin, 16)

            def cols(w, c):
                return w.rearrange("(k p) n -> p k n", p=P)[:, :, c * BIG:(c + 1) * BIG]

            for i in range(CH_A):
                sp.dma_start(ring[:, i, :, :], cols(w_mod[0], i)).then_inc(wa_in[i], 16)

            def ring_chunk(i, src):
                if i < 2:
                    sp.wait_ge(a_ps, i + 1)
                else:
                    sp.wait_ge(job[0], USED[i - 2])
                sp.dma_start(ring[:, i % 2, :, :], src).then_inc(wp_in[i % 2], 16)

            def bias_load(v):
                sp.dma_start(bias[v], bias_in[v]).then_inc(s_bias[v], 16)

            ring_chunk(0, cols(w_qkv, 2))
            ring_chunk(1, cols(w_qkv, 3))
            sp.wait_ge(job[0], JOB_H)
            bias_load(0)
            ring_chunk(2, cols(w_qkv, 4))
            ring_chunk(3, cols(w_qkv, 5))
            ring_chunk(4, cols(w_qkv, 0))
            ring_chunk(5, cols(w_qkv, 1))
            ring_chunk(6, cols(w_o, 0))
            ring_chunk(7, cols(w_o, 1))
            bias_load(1)
            sp.wait_ge(bias_used, 1)
            bias_load(2)
            sp.wait_ge(bias_used, 3)
            for L in range(DEPTH):
                if L:
                    sp.wait_ge(u_free[0], (NGRP + 1) * G)
                    sp.dma_start(dft_sb[0], dft_ch.rearrange("(k p) n -> p k n", p=P)).then_inc(wf_in[0], 16)
                    sp.dma_start(dft_sb[1], dft_pos.rearrange("(k p) n -> p k n", p=P)).then_inc(wf_in[1], 16)
                    sp.wait_ge(v_free[0], (NGRP + 1) * G)
                    for i in range(2):
                        sp.dma_start(ring[:, 2 + i, :, :], cols(w_fno, i)).then_inc(wf_in[2 + i], 16)
                for c4 in range(4):
                    if L == 0 and c4 == 1:
                        sp.wait_ge(at_ok, NT)
                    if L == 1:
                        if c4 == 0:
                            sp.wait_ge(job[L], 24)
                        elif c4 == 1:
                            sp.wait_ge(job[L], 32)
                        elif c4 == 3:
                            sp.wait_ge(o_ps[L], 2 * NT)
                    sp.dma_start(wq[:, c4, :, :], cols(w_query[L], c4)).then_inc(wq_in[L][c4], 16)
            sp.wait_ge(hT_ps[1], NT)
            sp.wait_ge(hc_ok[1], NT)
            sp.dma_start(hx_next, norm_fin).then_inc(wfin_in, 16)
            for t in range(NT):
                sp.wait_ge(f_out, t + 1)
                sp.dma_start(out[t * P:(t + 1) * P, :], xres[:, t, :]).then_inc(s_out, 16)
            sp.wait_ge(s_out, 16 * NT)

        @block.gpsimd
        def _(pool):
            pool.memset(ones[:], 1.0).then_inc(s_ones, 1)
            for m in range(NMACC):
                if m < 2:
                    pool.wait_ge(a_ps, CH_A)
                else:
                    pool.wait_ge(macc_ok, m - 1)
                L, i = (0, CH_A + m) if m < 2 * N_MOD - CH_A else (1, m - 2 * N_MOD + CH_A)
                pool.dma_start(ring[:, 2 + m % 2, :, :],
                               w_mod[L].rearrange("(k p) n -> p k n", p=P)[:, :, i * BIG:(i + 1) * BIG]
                               ).then_inc(wm_in[m % 2], 16)
            pool.wait_ge(macc_ok, NMACC)
            for i in range(2):
                ins = pool.memset(p_mid[i], 0.0)
            ins.then_inc(s_pads, 1)
            pool.wait_ge(ev_dve[0], (JOB_H + JOB_K + JOB_V + JOB_Q) // 2)
            pool.wait_ge(ev_act[0], (JOB_H + JOB_K + JOB_V + JOB_Q) // 2)
            for b in range(NT):
                def qcopy(j, nn, first=False):
                    if not first:
                        hold(pool, qf_ok[1], nn)
                    pool.tensor_copy(qpair, qT[:, j, b * P:(b + 1) * P]).then_inc(qp_ok, 1)
                    hold(pool, qp_ok, nn + 1)
                    for hh in range(2):
                        if not first:
                            hold(pool, sc_ps[hh], nn)
                        pool.tensor_scalar(qfix[hh], qpair, iota16[:, TOPK + hh:TOPK + hh + 1],
                                           None, ALU.mult).then_inc(qf_ok[hh], 1)

                qcopy(0, PAIRS * b, first=(b == 0))
                with pool.Fori(1, PAIRS) as j:
                    qcopy(j, j + PAIRS * b)

            for L in range(DEPTH):
                def gather(table, rows, b, g8, par, arrived):
                    pool.indirect_dma_start(out=rows[:, b, :], out_offset=None, in_=table,
                                            in_offset=bass.IndirectOffsetOnAxis(ap=idx[par][:, g8 + b:g8 + b + 1],
                                                                                axis=0)).then_inc(arrived[b], 16)

                def u_group(grp, off, par):
                    for b in range(G):
                        if b % 4 == 0:
                            hold(pool, u_free[L], G * grp + b + 4)
                        gather(peer_u[L], urows, b, off * G, par, u_in)

                def v_group(grp, off, par):
                    for b in range(G):
                        if b % 4 == 0:
                            hold(pool, v_free[L], G * grp + b + 4)
                        gather(peer_v[L], vrows, b, off * G, par, v_in)

                def pair(m, first):
                    for par in range(2):
                        hold(pool, idx_ok[L], 2 * m + par + 1)
                        if first and par == 0:
                            pool.wait_ge(o_ps[L], 2 * NT)
                        u_group(4 * m + 2 * par, 0, par)
                        if not (first and par == 0):
                            v_group(4 * m + 2 * par - 1, 1, 1 - par)
                        u_group(4 * m + 2 * par + 1, 1, par)
                        if first and par == 0:
                            pool.wait_ge(x_ok[L], NT)
                            pool.wait_ge(sq_done[L], NT + (NC if L == 0 else 0) + NT)
                        v_group(4 * m + 2 * par, 0, par)

                pair(0, True)
                with pool.Fori(1, NITEM // 2) as m:
                    pair(m, False)
                v_group(NGRP - 1, 1, 1)

        @block.tensor
        def _(pe):
            pe.wait_ge(s_small, 16 * NSMALL)
            pe.wait_ge(s_ones, 1)
            pe.wait_ge(s_silu, 1)
            for L in range(DEPTH):
                n = [0]

                def bank():
                    i = n[0]
                    if i >= 4:
                        pe.wait_ge((ev_dve if i % 2 == 0 else ev_act)[L], (i - 4) // 2 + 1)
                    return ps[:, i % 4, :]

                def done(ins):
                    ins.then_inc(job[L], 1)
                    n[0] += 1
                    if L == 0:
                        for m in sums_after.get(n[0] - 4, []):
                            mod_cols(m)

                def mod_cols(m):
                    pe.wait_ge(macc_ok, m + 1)
                    for blk in range(4):
                        at = 2 * 4 * CH_A + 4 * m + blk
                        ins = pe.matmul(ps[:, 7, at:at + 1], macc[m % 2][:, blk * P:(blk + 1) * P], ones[:, 0:1],
                                        start=True, stop=True)
                    ins.then_inc(mcol_ps, 1)

                def ring_wait(i):
                    pe.wait_ge(wp_in[i % 2], 16 * (i // 2 + 1))
                    return ring[:, i % 2, :, :]

                if L == 0:
                    def turn_row(i):
                        pe.wait_ge(arow_ok, i + 1)
                        for blk in range(4):
                            j = 4 * i + blk
                            ins = pe.transpose(ps[:, 7, 2 * j:2 * j + 2], arow[i % 2][:, blk * P:(blk + 1) * P],
                                               ident[0:2, 0:2])
                        ins.then_inc(acol_ps, 1)

                    for i in range(CH_A):
                        pe.wait_ge(wa_in[i], 16)
                        for k in range(KD):
                            ins = pe.matmul(ps[0:2, 4 + i % 2, :], silu[:, k, :], ring[:, i, k, :],
                                            start=(k == 0), stop=(k == KD - 1))
                        ins.then_inc(a_ps, 1)
                        if i:
                            turn_row(i - 1)
                    turn_row(CH_A - 1)
                else:
                    pe.wait_ge(hT_ok[L - 1], 2 * NT)
                pe.wait_ge(xn_ok[L], NT + (NC if L == 0 else 0))
                if L:
                    pe.wait_ge(y_ok[L - 1], NT + 1)
                    pe.wait_ge(qT_ok[L - 1], NITEM)
                for k in range(KD):
                    dst = bank()
                    for t in range(NT):
                        ins = pe.transpose(dst[:, t * P:(t + 1) * P], [xn, xn1][L][:, t, k * P:(k + 1) * P], ident[:])
                    done(ins)
                if L == 0:
                    for k2 in range(KD // 2):
                        dst = bank()
                        for kk in range(2):
                            for t in range(NC):
                                k = 2 * k2 + kk
                                ins = pe.transpose(dst[:, (2 * kk + t) * P:(2 * kk + t + 1) * P],
                                                   xctx[:, t, k * P:(k + 1) * P], ident[:])
                        done(ins)
                    pe.wait_ge(ev_dve[L], n[0] // 2)
                    pe.wait_ge(ev_act[L], n[0] // 2)
                    c = 0
                    for i in range(2):
                        w = ring_wait(c)
                        for blk in range(4):
                            for src, width in ((hT, SEQ), (hcT, CTX)):
                                dst = bank()
                                for k in range(KD):
                                    ins = pe.matmul(dst[:, 0:width], w[:, k, blk * P:(blk + 1) * P], src[:, k, :],
                                                    start=(k == 0), stop=(k == KD - 1))
                                done(ins)
                        c += 1
                    for i in range(2):
                        w = ring_wait(c)
                        for t in range(NT + NC):
                            dst = bank()
                            for k in range(KD):
                                lhs = hT[:, k, t * P:(t + 1) * P] if t < NT else hcT[:, k, (t - NT) * P:(t - NT + 1) * P]
                                ins = pe.matmul(dst, lhs, w[:, k, :], start=(k == 0), stop=(k == KD - 1))
                            done(ins)
                        c += 1
                    for i in range(2):
                        w = ring_wait(c)
                        for blk in range(4):
                            dst = bank()
                            for k in range(KD):
                                ins = pe.matmul(dst, w[:, k, blk * P:(blk + 1) * P], hT[:, k, :],
                                                start=(k == 0), stop=(k == KD - 1))
                            done(ins)
                        c += 1
                else:
                    pe.wait_ge(ev_dve[L], n[0] // 2)
                    pe.wait_ge(ev_act[L], n[0] // 2)
                    pe.wait_ge(wf_in[0], 16)
                    w = dft_sb[0]
                    for t in range(NT):
                        for g in range(4):
                            dst = bank()
                            for kk in range(2):
                                ins = pe.matmul(dst, hT[:, 2 * g + kk, t * P:(t + 1) * P], w[:, kk, :],
                                                start=(kk == 0), stop=(kk == 1))
                            done(ins)
                    pe.wait_ge(ev_dve[L], n[0] // 2)
                    pe.wait_ge(ev_act[L], n[0] // 2)
                    pe.wait_ge(wf_in[1], 16)
                    w = dft_sb[1]
                    for j in range(KD):
                        dst = bank()
                        for i in range(8):
                            part, t = i // NT, i % NT
                            at = part * 256 + (j % 2) * P
                            ins = pe.matmul(dst, cs[:, t, j // 2, at:at + P], w[:, i, :], start=(i == 0), stop=(i == 7))
                        done(ins)
                if L == 0:
                    for m in sums_after[JOB_H + JOB_K + JOB_V + JOB_Q - 2]:
                        mod_cols(m)
                for v in range(4):
                    pe.wait_ge(dg_ok[L], v + 1)
                    for half in range(2):
                        dst = bank()
                        done(pe.matmul(dst, ones[:], modb[:, v, half * 512:(half + 1) * 512], start=True, stop=True))
                pe.wait_ge(ev_dve[L], n[0] // 2)
                pe.wait_ge(ev_act[L], n[0] // 2)

                if L == 0:
                    wout = [ring_wait(6), ring_wait(7)]
                else:
                    pe.wait_ge(wf_in[2], 16)
                    pe.wait_ge(wf_in[3], 16)
                    wout = [ring[:, 2, :, :], ring[:, 3, :, :]]

                def out_proj(t, half, lhs):
                    for k in range(KD):
                        ins = pe.matmul(ps[:, OUT_BANK[L][t] + half, :], lhs(k), wout[half][:, k, :],
                                        start=(k == 0), stop=(k == KD - 1))
                    ins.then_inc(o_ps[L], 1)

                def turn_h(nt):
                    pe.wait_ge(hn_ok[L], nt + 1)
                    for k in range(KD):
                        ins = pe.transpose(ps[:, 6 + k // 4, (k % 4) * P:(k % 4 + 1) * P],
                                           hx_next[:, k * P:(k + 1) * P], ident[:])
                    ins.then_inc(hT_ps[L], 1)

                def head_scores(chunk, i, par, first=False):
                    if not first:
                        pe.wait_ge(q_ok[L], i)
                    for k in range(KD):
                        ins = pe.matmul(ps[:, 2, 0:256], hxT[:, k, :], wq[:, chunk, k, par * 256:(par + 1) * 256],
                                        start=(k == 0), stop=(k == KD - 1))
                    ins.then_inc(q_ps[L], 1)
                    pe.wait_ge(q_ok[L], i + 1)
                    for a in range(2):
                        ins = pe.transpose(ps[:, 3, a * P:(a + 1) * P], q_sb[:, a * P:(a + 1) * P], ident[:])
                    ins.then_inc(qT_ps[L], 1)
                    pe.wait_ge(qT_ok[L], i + 1)
                    pe.wait_ge(s_read[L], i + 1)
                    for a in range(2):
                        ins = pe.matmul(ps[:, 4 + par, a * P:(a + 1) * P], qT_sb[:, a, :], keys[:, L, a, :],
                                        start=True, stop=True)
                    ins.then_inc(s_ps[L], 1)

                def first_scores():
                    pe.wait_ge(hT_ok[L], 2)
                    pe.wait_ge(wq_in[L][0], 16)
                    pe.wait_ge(x_ok[L], NT - 1 if L == 0 else 2)
                    head_scores(0, 0, 0, first=True)

                if L == 0:
                    pe.wait_ge(s_pads, 1)

                    def scores(b, j, hh, nn):
                        hold(pe, qf_ok[hh], nn + 1)
                        pe.matmul(ps[:, hh, 0:WIN], qfix[hh], kT[:, j, WSTART[b]:WSTART[b] + WIN], start=True, stop=True)
                        pe.matmul(ps[:, hh, WIN:WIN + CTX], qfix[hh], kcT[:, j, :],
                                  start=True, stop=True).then_inc(sc_ps[hh], 1)

                    def turn(b, hh, nn):
                        prob = (p_mid if VARIANT[b] == 1 else p_edge)[hh]
                        pe.wait_ge(exp_ok[hh], nn + 1)
                        if VARIANT[b] == 1:
                            pe.transpose(ps[:, 4 + hh, 0:P], prob[:, 4 * P:5 * P], ident[:])
                        for i in range(4):
                            ins = pe.transpose(ps[:, 2 + hh, i * P:(i + 1) * P], prob[:, i * P:(i + 1) * P], ident[:])
                        ins.then_inc(pt_ps[hh], 1)

                    def values(b, j, hh, nn):
                        first = WSTART[b] // P
                        tiles = list(range(first, first + (3 if VARIANT[b] == 1 else 2))) + [NT, NT + 1]
                        hold(pe, pt_act[hh], nn + 1)
                        if VARIANT[b] == 1:
                            pe.wait_ge(pt_dve[hh], nn - PAIRS + 1)
                        dst = ps[:, 6:8, :].rearrange("p a n -> p (a n)")
                        for i, tile in enumerate(tiles):
                            ins = pe.matmul(dst[:, bass.ds((2 * j + hh) * DH, DH)], pT[hh][:, i * P:(i + 1) * P],
                                            vtok[:, tile, bass.ds((2 * j + hh) * DH, DH)],
                                            start=(i == 0), stop=(i == len(tiles) - 1))
                        ins.then_inc(pv_ok[hh], 1)

                    scores(0, 0, 0, 0)
                    scores(0, 0, 1, 0)
                    for b in range(NT):
                        base = b * PAIRS
                        if b:
                            pe.wait_ge(x_ok[L], b)
                        turn(b, 0, base)
                        with pe.Fori(0, PAIRS - 1) as j:
                            scores(b, j + 1, 0, j + 1 + base)
                            turn(b, 1, j + base)
                            values(b, j, 0, j + base)
                            scores(b, j + 1, 1, j + 1 + base)
                            turn(b, 0, j + 1 + base)
                            values(b, j, 1, j + base)
                        last = base + PAIRS - 1
                        turn(b, 1, last)
                        values(b, PAIRS - 1, 0, last)
                        values(b, PAIRS - 1, 1, last)
                        if b < NT - 1:
                            scores(b + 1, 0, 0, last + 1)
                            scores(b + 1, 0, 1, last + 1)
                        pe.wait_ge(at_ok, b + 1)
                        for k in range(KD):
                            ins = pe.transpose(ps[:, 2 + k // 4, (k % 4) * P:(k % 4 + 1) * P],
                                               attn[:, k * P:(k + 1) * P], ident[:])
                        ins.then_inc(atT_ps, 1)
                        if b == NT - 1:
                            turn_h(0)
                        pe.wait_ge(atT_ok, b + 1)
                        out_proj(b, 0, lambda k: attnT[:, k, :])
                        if b == NT - 1:
                            first_scores()
                        out_proj(b, 1, lambda k: attnT[:, k, :])
                else:
                    for t in range(NT):
                        if t == 2:
                            turn_h(0)
                            pe.wait_ge(x_ok[L], 1)
                        if t == 3:
                            first_scores()
                        for half in range(2):
                            out_proj(t, half, lambda k: fT[:, k, t * P:(t + 1) * P])

                def add_rows(grp, start):
                    for b in range(G):
                        pe.wait_ge(dg_in[L], G * grp + b + 1)
                        pe.wait_ge(v_in[b], 16 * grp + 16 * (NGRP * L + 1))
                        for half in range(2):
                            ins = pe.matmul(ps[:, half, :], diag[:, b, :], vrows[:, b, half * 512:(half + 1) * 512],
                                            start=(start and b == 0), stop=False, skip_group_check=True)
                        ins.then_inc(v_free[L], 1)

                def pair(m, next_chunk, tile_start, chain=True):
                    for par in range(2):
                        add_rows(4 * m + 2 * par, tile_start and par == 0)
                        if chain:
                            head_scores(next_chunk, 2 * m + par + 2, par)
                        add_rows(4 * m + 2 * par + 1, False)

                def tile(t, last):
                    hold(pe, y_ok[L], t + 1)
                    pair(NPAIR_T * t, 1, True)
                    with pe.Fori(1, NPAIR_T - 1) as pr:
                        pair(NPAIR_T * t + pr, pr + 1, False)
                    if not last:
                        turn_h(t + 1)
                        hold(pe, hT_ok[L], 2 * t + 4)
                    pair(NPAIR_T * t + NPAIR_T - 1, 0, False, chain=not last)

                pe.sem_inc(v_free[L], G)
                head_scores(0, 1, 1)
                pe.wait_ge(x_ok[L], NT)
                for c4 in range(1, 4):
                    pe.wait_ge(wq_in[L][c4], 16)
                tile(0, False)
                with pe.Fori(1, NT - 1) as t:
                    tile(t, False)
                tile(NT - 1, True)

        @block.scalar
        def _(act):
            act.wait_ge(s_small, 16 * NSMALL)
            act.activation(silu[:], craw[:], ACT.Silu).then_inc(s_silu, 1)
            act.wait_ge(s_x, 16 * NT)
            act.wait_ge(s_ctxin, 16 * NC)
            for L in range(DEPTH):
                tiles = [xres[:, t, :] for t in range(NT)] + ([xctx[:, t, :] for t in range(NC)] if L == 0 else [])

                def square(t, n):
                    act.wait_ge(sq_done[L], n)
                    act.activation(sqjs[L], xres[:, t, :], ACT.Square, accum_out=ss[:, t:t + 1]).then_inc(sq_done[L], 1)

                def root(t0, t1, k):
                    act.wait_ge(var_ok[L], k)
                    act.activation(rstd[:, t0:t1], ss[:, t0:t1], ACT.Sqrt).then_inc(std_ok[L], 1)

                if L == 0:
                    for i, src in enumerate(tiles):
                        act.activation(xn[:, 0, :], src, ACT.Square,
                                       accum_out=ss[:, i:i + 1]).then_inc(sq_done[L], 1)
                        act.wait_ge(sq_done[L], i + 1)
                    root(0, len(tiles), 1)
                    act.wait_ge(rstd_ok[L], 1)
                    for i, src in enumerate(tiles):
                        dst = xn[:, i, :] if i < NT else src
                        act.activation(dst, src, ACT.Copy, scale=rstd[:, i:i + 1]).then_inc(xn_ok[L], 1)
                else:
                    act.wait_ge(rstd_ok[L], 2)
                    act.activation(xn1[:, NT - 1, :], xres[:, NT - 1, :], ACT.Copy,
                                   scale=rstd[:, NT - 1:NT]).then_inc(xn_ok[L], 1)

                def evac(i, outs, ins_, scales=None, shifts=None, scale=1.0):
                    if i % 2 == 0:
                        return
                    act.wait_ge(job[L], i + 1)
                    for q, (o, s) in enumerate(zip(outs, ins_)):
                        if scales is not None:
                            ins = act.activation(o, s, ACT.Identity, bias=shifts[q], scale=scales[q])
                        else:
                            ins = act.activation(o, s, ACT.Copy, scale=scale)
                    ins.then_inc(ev_act[L], 1)

                def turned_h(nt):
                    act.wait_ge(hT_ps[L], nt + 1)
                    for a in range(2):
                        act.activation(hxT[:, 4 * a:4 * a + 4, :], ps[:, 6 + a, :].rearrange("p (k n) -> p k n", k=4),
                                       ACT.Copy).then_inc(hT_ok[L], 1)

                act.wait_ge(mod_ok[L], 1)
                dense_copies(L, evac, ps, modc[L], a_mix[L], hT, hcT, kT, kcT, vtok, qT, cs, fT, modb)

                if L == 0:
                    def soft(b, hh, nn, h):
                        prob = p_edge[hh].rearrange("p (a n) -> p a n", a=2)
                        if VARIANT[b] == 1:
                            prob = p_mid[hh].rearrange("p (a n) -> p a n", a=2)[:, :, 64:64 + WIN]
                        act.wait_ge(nmx_ok[hh], nn + 1)
                        act.activation(prob, ps[:, hh, :].rearrange("p (a n) -> p a n", a=2), ACT.Exp,
                                       bias=nmx[:, hh:hh + 1], accum_out=esum[:, h]).then_inc(exp_ok[hh], 1)

                    def turned(hh, nn):
                        act.wait_ge(pt_ps[hh], nn + 1)
                        act.activation(pT[hh][:, 0:512], ps[:, 2 + hh, :], ACT.Copy).then_inc(pt_act[hh], 1)

                    act.wait_ge(s_pads, 1)
                    for b in range(NT):
                        base = b * PAIRS
                        if b == 0:
                            soft(0, 0, 0, slice(0, 1))
                            soft(0, 1, 0, slice(1, 2))
                        turned(0, base)
                        with act.Fori(0, PAIRS - 1) as j:
                            turned(1, j + base)
                            soft(b, 0, j + 1 + base, bass.ds(2 * j + 2, 1))
                            turned(0, j + 1 + base)
                            soft(b, 1, j + 1 + base, bass.ds(2 * j + 3, 1))
                        turned(1, base + PAIRS - 1)
                        if b == NT - 1:
                            root(0, 1, 2)
                        if b < NT - 1:
                            act.wait_ge(at_chain, b + 1)
                            soft(b + 1, 0, base + PAIRS, slice(0, 1))
                            soft(b + 1, 1, base + PAIRS, slice(1, 2))
                        act.wait_ge(atT_ps, b + 1)
                        act.activation(attnT, ps[:, 2:4, :].rearrange("p a (k n) -> p (a k) n", k=4),
                                       ACT.Copy).then_inc(atT_ok, 1)
                        if b < NT - 1:
                            act.wait_ge(x_ok[L], b + 1)
                            square(b, len(tiles) + b)
                else:
                    for t in range(NT - 1):
                        act.wait_ge(x_ok[L], t + 1)
                        square(t, len(tiles) + t)
                        if t == 0:
                            root(0, 1, 3)
                        if t == 0:
                            turned_h(0)
                def query_copies(i):
                    act.wait_ge(q_ps[L], i + 1)
                    act.activation(q_sb, ps[:, 2, 0:256], ACT.Copy).then_inc(q_ok[L], 1)
                    act.wait_ge(qT_ps[L], i + 1)
                    act.activation(qT_sb, ps[:, 3, 0:256].rearrange("p (a n) -> p a n", a=2),
                                   ACT.Copy).then_inc(qT_ok[L], 1)

                def gate_exp(i, par):
                    act.wait_ge(top_ok[L], i + 1)
                    act.activation(gate_e[par][:], tops, ACT.Exp, bias=gneg[:],
                                   accum_out=gsum[:]).then_inc(gexp_ok[L], 1)

                def gelu(grp, gp):
                    act.wait_ge(u_free[L], G * grp + 2 * G)
                    act.activation(gel[:, gp, :], pre[:, gp, :], ACT.Gelu).then_inc(gel_ok[L], 1)

                def diags(grp, gp):
                    act.wait_ge(w_ok[L], grp + 1)
                    for b in range(G):
                        act.wait_ge(v_free[L], G * grp + b + 1)
                        act.activation(diag[:, b, :], ident[:], ACT.Copy,
                                       scale=wgt[:, gp, b:b + 1]).then_inc(dg_in[L], 1)

                def next_square(t):
                    act.wait_ge(sq_done[L + 1], t)
                    act.activation(ps[:, 6:8, :].rearrange("p a n -> p (a n)"), xres[:, t, :], ACT.Square,
                                   accum_out=ss[:, t:t + 1]).then_inc(sq_done[L + 1], 1)

                def next_root(t0, t1, k):
                    act.wait_ge(var_ok[L + 1], k)
                    act.activation(rstd[:, t0:t1], ss[:, t0:t1], ACT.Sqrt).then_inc(std_ok[L + 1], 1)

                def pair(m, chain=True, last=False):
                    for par in range(2):
                        if last and par == 1:
                            next_root(0, NT - 1, 1)
                        g0 = 4 * m + 2 * par
                        gelu(g0, 0)
                        diags(g0, 0)
                        if chain:
                            query_copies(2 * m + par + 2)
                        gelu(g0 + 1, 1)
                        if not (last and par == 1):
                            gate_exp(2 * m + par + 1, 1 - par)
                        diags(g0 + 1, 1)

                def tile(t, last):
                    with act.Fori(0, NPAIR_T - 1) as pr:
                        pair(NPAIR_T * t + pr)
                    if not last:
                        turned_h(t + 1)
                    else:
                        act.wait_ge(y_read[L], NT)
                        for tt in range(NT - 1):
                            next_square(tt)
                    pair(NPAIR_T * t + NPAIR_T - 1, chain=not last, last=last)
                    if last and L == 0:
                        act.wait_ge(rstd_ok[1], 1)
                        act.wait_ge(s_ps[0], NITEM)
                        for tt in range(NT - 1):
                            act.activation(xn1[:, tt, :], xres[:, tt, :], ACT.Copy,
                                           scale=rstd[:, tt:tt + 1]).then_inc(xn_ok[1], 1)
                    act.wait_ge(v_free[L], G * 2 * PH * (t + 1) + G)
                    act.wait_ge(y_read[L], t + 1)
                    act.activation(ytmp, ps[:, 0:2, :].rearrange("p a n -> p (a n)"), ACT.Copy).then_inc(y_ok[L], 1)

                act.sem_inc(y_ok[L], 1)
                if L == 0:
                    turned_h(0)
                query_copies(0)
                gate_exp(0, 0)
                query_copies(1)
                act.wait_ge(x_ok[L], NT)
                square(NT - 1, len(tiles) + NT - 1)
                root(1, NT, 3 + L)
                tile(0, False)
                with act.Fori(1, NT - 1) as t:
                    tile(t, False)
                tile(NT - 1, True)
                act.wait_ge(y_read[L], NT + 1)
                next_square(NT - 1)
                next_root(NT - 1, NT, 2)

        @block.vector
        def _(dve):
            dve.wait_ge(s_small, 16 * NSMALL)
            for L in range(DEPTH):
                ch = Count(dve, dchain[L])
                nt_ln = NT + (NC if L == 0 else 0)

                def mean(t0, t1, ln, squares):
                    dve.wait_ge(sq_done[ln], squares)
                    dve.tensor_scalar(ss[:, t0:t1], ss[:, t0:t1], 1.0 / D, EPS, ALU.mult, ALU.add).then_inc(var_ok[ln], 1)

                def inverse(t0, t1, ln, k):
                    dve.wait_ge(std_ok[ln], k)
                    dve.reciprocal(rstd[:, t0:t1], rstd[:, t0:t1]).then_inc(rstd_ok[ln], 1)
                    dve.wait_ge(rstd_ok[ln], k)

                if L == 0:
                    mean(0, nt_ln, 0, nt_ln)
                    inverse(0, nt_ln, 0, 1)
                if L == 0:
                    for i in range(CH_A):
                        dve.wait_ge(a_ps, i + 1)
                        if i >= 2:
                            dve.wait_ge(acol_ps, i - 1)
                        dve.tensor_copy(arow[i % 2], ps[0:2, 4 + i % 2, :]).then_inc(arow_ok, 1)
                    nA = 4 * CH_A
                    dve.wait_ge(acol_ps, CH_A)
                    ch.step(dve.tensor_tensor(modc[0][:, 0:nA, :], ps[:, 7, 0:2 * nA].rearrange("p (j n) -> p j n", n=2),
                                              bmod[:, 0, 0:nA].unsqueeze(2).to_broadcast([P, nA, 2]), ALU.add))
                    ch.step(dve.tensor_scalar(a_mix[0][:], modc[0][:, KD:2 * KD, :], 1.0, None, ALU.add))
                    dve.tensor_tensor(a_mix[0][:], a_mix[0][:], norms[:, 0, :].unsqueeze(2).to_broadcast([P, KD, 2]),
                                      ALU.mult).then_inc(mod_ok[L], 1)
                    dve.wait_ge(mod_ok[L], 1)

                mc = Count(dve, macc_c)

                def mod_sum(m):
                    w = ring[:, 2 + m % 2, :, :]
                    dve.wait_ge(wm_in[m % 2], 16 * (m // 2 + 1))
                    if m >= 2:
                        dve.wait_ge(mcol_ps, m - 1)
                    mc.step(dve.tensor_scalar(macc[m % 2], w[:, 0, :], silu[:, 0, 0:1], None, ALU.mult))
                    for k in range(1, KD):
                        ins = dve.scalar_tensor_tensor(macc[m % 2], w[:, k, :], silu[:, k, 0:1], macc[m % 2],
                                                       ALU.mult, ALU.add)
                        if k < KD - 1:
                            mc.step(ins)
                    ins.then_inc(macc_ok, 1)

                def evac(i, outs, ins_, scales=None, shifts=None, scale=1.0):
                    if i % 2:
                        return
                    dve.wait_ge(job[L], i + 1)
                    for q, (o, s) in enumerate(zip(outs, ins_)):
                        if scales is not None:
                            ins = dve.tensor_scalar(o, s, scales[q], shifts[q], ALU.mult, ALU.add)
                        elif scale != 1.0:
                            ins = dve.tensor_scalar(o, s, scale, None, ALU.mult)
                        else:
                            ins = dve.tensor_copy(o, s)
                    ins.then_inc(ev_dve[L], 1)
                    if L == 0:
                        for m in sums_after.get(i, []):
                            mod_sum(m)

                def mod_b():
                    if L == 0:
                        dve.wait_ge(mcol_ps, NMACC)
                        at = 2 * nA
                        ch.step(dve.tensor_tensor(modc[0][:, nA:MODB, 0], ps[:, 7, at:at + MODB - nA],
                                                  bmod[:, 0, nA:MODB], ALU.add))
                        at += MODB - nA
                        ch.step(dve.tensor_tensor(modc[1][:, :, 0], ps[:, 7, at:at + MODB], bmod[:, 1, :], ALU.add))
                        for l in range(DEPTH):
                            ch.step(dve.tensor_scalar(a_ffn[l][:], modc[l][:, 4 * KD:5 * KD, 0], 1.0, None, ALU.add))
                            ch.step(dve.tensor_tensor(a_ffn[l][:], a_ffn[l][:], norms[:, DEPTH + l, :], ALU.mult))
                        ch.step(dve.tensor_scalar(a_mix[1][:, :, 0], modc[1][:, KD:2 * KD, 0], 1.0, None, ALU.add))
                        dve.tensor_tensor(a_mix[1][:, :, 0], a_mix[1][:, :, 0], norms[:, 1, :], ALU.mult).then_inc(mod_ok[1], 1)
                        dve.wait_ge(mod_ok[1], 1)
                    for v, col in ((AF, a_ffn[L][:]), (SHF, modc[L][:, 3 * KD:4 * KD, 0]),
                                   (GF, modc[L][:, 5 * KD:6 * KD, 0]), (GM, modc[L][:, 2 * KD:3 * KD, 0])):
                        dve.tensor_tensor(modb[:, v, :].rearrange("p (k n) -> p k n", k=KD),
                                          ident[:, :].unsqueeze(1).to_broadcast([P, KD, P]),
                                          col.unsqueeze(2).to_broadcast([P, KD, P]), ALU.mult).then_inc(dg_ok[L], 1)

                jobs = dense_copies(L, evac, ps, modc[L], a_mix[L], hT, hcT, kT, kcT, vtok, qT, cs, fT, modb, mod_b)
                dve.wait_ge(ev_act[L], jobs // 2)

                def residual(t):
                    dve.wait_ge(o_ps[L], 2 * t + 2)
                    b0 = OUT_BANK[L][t]
                    ch.step(dve.tensor_tensor(otmps[L], ps[:, b0:b0 + 2, :].rearrange("p a n -> p (a n)"),
                                              modb[:, GM, :], ALU.mult))
                    dve.tensor_tensor(xres[:, t, :], xres[:, t, :], otmps[L], ALU.add).then_inc(x_ok[L], 1)
                    dve.wait_ge(x_ok[L], t + 1)

                def prep(t, col):
                    dve.scalar_tensor_tensor(hx_next, xres[:, t, :], rstd[:, col], modb[:, AF, :],
                                             ALU.mult, ALU.mult).then_inc(hn_chain[L], 1)
                    hold(dve, hn_chain[L], t + 1)
                    dve.tensor_tensor(hx_next, hx_next, modb[:, SHF, :], ALU.add).then_inc(hn_ok[L], 1)

                def take_h(t):
                    hold(dve, hn_ok[L], t + 1)
                    hold(dve, u_free[L], 2 * PH * G * t + G)
                    dve.tensor_copy(hx_cur, hx_next).then_inc(hc_ok[L], 1)
                    hold(dve, hc_ok[L], t + 1)

                def dots(grp, gp):
                    for b in range(G):
                        dve.wait_ge(u_in[b], 16 * grp + 16 * (NGRP * L + 1))
                        dve.tensor_tensor_reduce(urows[:, b, :], urows[:, b, :], hx_cur, 1.0, 0.0, ALU.mult, ALU.add,
                                                 pre[:, gp, b:b + 1]).then_inc(u_free[L], 1)

                def weights(grp, gp, par):
                    hold(dve, gel_ok[L], grp + 1)
                    dve.scalar_tensor_tensor(wgt[:, gp, :], gel[:, gp, :], gate_r[par][:],
                                             gate_e[par][:, gp * G:(gp + 1) * G],
                                             ALU.mult, ALU.mult).then_inc(w_ok[L], 1)

                def halves(i, par):
                    ct = Count(dve, tk[L], KSTEPS * i)
                    score = [ps[:, 4 + par, a * P:(a + 1) * P] for a in range(2)]
                    hold(dve, s_ps[L], i + 1)
                    dve.max(topv[:, 0, 0:8], score[0])
                    ct.step(dve.max(topv[:, 1, 0:8], score[1]))
                    for a in range(2):
                        dve.match_replace(wk[:, a, :], topv[:, a, 0:8], score[a], NEG)
                    dve.max_index(ixu[:, 0, 0:8], topv[:, 0, 0:8], score[0])
                    dve.max_index(ixu[:, 1, 0:8], topv[:, 1, 0:8], score[1]).then_inc(s_read[L], 1)
                    hold(dve, s_read[L], i + 3)
                    dve.max(topv[:, 0, 8:16], wk[:, 0, :])
                    ct.step(dve.max(topv[:, 1, 8:16], wk[:, 1, :]))
                    dve.max_index(ixu[:, 0, 8:16], topv[:, 0, 8:16], wk[:, 0, :])
                    ct.step(dve.max_index(ixu[:, 1, 8:16], topv[:, 1, 8:16], wk[:, 1, :]))
                    dve.tensor_tensor(cand.rearrange("p (a b) -> p a b", a=TOPK),
                                      topv[:, 0, :].unsqueeze(2).to_broadcast([P, TOPK, TOPK]),
                                      topv[:, 1, :].unsqueeze(1).to_broadcast([P, TOPK, TOPK]), ALU.add)
                    dve.tensor_scalar(tab[:, 0, :], ixu[:, 0, :], float(NKEY), None, ALU.mult)
                    ct.step(dve.tensor_copy(tab[:, 1, :], ixu[:, 1, :]))
                    return ct

                def choose(i, par, ct):
                    ct.step(dve.max(tops[:, 0:8], cand))
                    dve.match_replace(cand2, tops[:, 0:8], cand, NEG)
                    ct.step(dve.max_index(pos[:, 0:8], tops[:, 0:8], cand))
                    dve.tensor_scalar(gneg[:], tops[:, 0:1], -1.0, None, ALU.mult)
                    dve.max(tops[:, 8:16], cand2).then_inc(top_ok[L], 1)
                    hold(dve, top_ok[L], i + 1)
                    ct.step(dve.max_index(pos[:, 8:16], tops[:, 8:16], cand2))
                    dve.tensor_scalar(poshl[:, :, 0], pos[:], 4, None, ALU.logical_shift_right)
                    ct.step(dve.tensor_scalar(poshl[:, :, 1], pos[:], TOPK - 1, None, ALU.bitwise_and))
                    oh = onehot.rearrange("p (k a n) -> p k a n", k=TOPK, a=2)
                    ct.step(dve.tensor_tensor(oh, poshl[:, :, :].unsqueeze(3).to_broadcast([P, TOPK, 2, TOPK]),
                                              iota16[:, 0:TOPK].unsqueeze(1).unsqueeze(1).to_broadcast([P, TOPK, 2, TOPK]),
                                              ALU.is_equal))
                    ct.step(dve.tensor_tensor(oh, oh, tab.unsqueeze(1).to_broadcast([P, TOPK, 2, TOPK]), ALU.mult))
                    if not isinstance(i, int) or i > 0:
                        hold(dve, v_free[L], 2 * G * i - G)
                    ct.step(dve.tensor_reduce(expert[:], onehot.rearrange("p (k n) -> p k n", k=TOPK), AX.X, ALU.add))
                    dve.tensor_copy(idx[par][:], expert[:]).then_inc(idx_ok[L], 1)
                    hold(dve, gexp_ok[L], i + 1)
                    ct.step(dve.reciprocal(gate_r[par][:], gsum[:]))
                    assert ct.n == KSTEPS, ct.n

                def first_h():
                    dve.sem_inc(u_free[L], G)
                    dve.sem_inc(s_read[L], 2)
                    dve.sem_inc(y_read[L], 1)
                    prep(0, slice(0, 1))
                    take_h(0)

                if L == 0:
                    def masked(b, hh, nn, h):
                        hold(dve, sc_ps[hh], nn + 1)
                        dve.tensor_tensor(ps[:, hh, 0:WIN], ps[:, hh, 0:WIN], bias[VARIANT[b]][:, h, :],
                                          ALU.add).then_inc(lat_ok[hh], 1)
                        hold(dve, lat_ok[hh], nn + 1)
                        dve.tensor_reduce(nmx[:, hh:hh + 1], ps[:, hh, :], AX.X, ALU.max,
                                          negate=True).then_inc(nmx_ok[hh], 1)

                    def turned(b, hh, nn):
                        if VARIANT[b] == 1:
                            hold(dve, pt_ps[hh], nn + 1)
                            dve.tensor_copy(pT[hh][:, 512:640], ps[:, 4 + hh, 0:P]).then_inc(pt_dve[hh], 1)

                    dve.wait_ge(s_bias[0], 16)
                    masked(0, 0, 0, slice(0, 1))
                    masked(0, 1, 0, slice(1, 2))
                    for b in range(NT):
                        base = b * PAIRS
                        turned(b, 0, base)
                        with dve.Fori(0, PAIRS - 1) as j:
                            masked(b, 0, j + 1 + base, bass.ds(2 * j + 2, 1))
                            turned(b, 1, j + base)
                            masked(b, 1, j + 1 + base, bass.ds(2 * j + 3, 1))
                            turned(b, 0, j + 1 + base)
                        turned(b, 1, base + PAIRS - 1)
                        if b == NT - 1:
                            mean(0, 1, L, nt_ln + 1)
                        dve.wait_ge(nmx_ok[1], base + PAIRS)
                        dve.sem_inc(bias_used, 1)
                        dve.wait_ge(exp_ok[1], base + PAIRS)
                        dve.reciprocal(einv[:], esum[:]).then_inc(at_chain, 1)
                        dve.wait_ge(at_chain, b + 1)
                        dve.wait_ge(pv_ok[1], base + PAIRS)
                        dve.tensor_tensor(attn.rearrange("p (h n) -> p h n", h=HEADS),
                                          ps[:, 6:8, :].rearrange("p a (h n) -> p (a h) n", h=PAIRS),
                                          einv[:].unsqueeze(2).to_broadcast([P, HEADS, DH]), ALU.mult).then_inc(at_ok, 1)
                        if b < NT - 1:
                            dve.wait_ge(s_bias[VARIANT[b + 1]], 16)
                            masked(b + 1, 0, base + PAIRS, slice(0, 1))
                            masked(b + 1, 1, base + PAIRS, slice(1, 2))
                        if b < NT - 1:
                            residual(b)
                    inverse(0, 1, L, 2)
                    first_h()
                else:
                    residual(0)
                    mean(0, 1, L, nt_ln + 1)
                    inverse(0, 1, L, 3)
                    first_h()
                    residual(1)
                    residual(2)
                choose(0, 0, halves(0, 0))
                residual(NT - 1)
                mean(1, NT, L, nt_ln + NT)
                inverse(1, NT, L, 3 + L)

                def pair(m, last=False):
                    for par in range(2):
                        if last and par == 1:
                            mean(0, NT - 1, L + 1, NT - 1)
                        i = 2 * m + par
                        more = not (last and par == 1)
                        dots(2 * i, 0)
                        if more:
                            ct = halves(i + 1, 1 - par)
                        weights(2 * i, 0, par)
                        dots(2 * i + 1, 1)
                        if last and par == 1:
                            inverse(0, NT - 1, L + 1, 1)
                        if more:
                            choose(i + 1, 1 - par, ct)
                        weights(2 * i + 1, 1, par)

                def final_norm(t):
                    dve.scalar_tensor_tensor(xres[:, t, :], xres[:, t, :], rstd[:, t:t + 1], hx_next, ALU.mult,
                                             ALU.mult).then_inc(f_out, 1)

                def finish(t):
                    hold(dve, y_ok[L], t + 2)
                    dve.tensor_tensor(ytmp, ytmp, modb[:, GF, :], ALU.mult).then_inc(fchain[L], 1)
                    hold(dve, fchain[L], t + 1)
                    dve.tensor_tensor(xres[:, t, :], xres[:, t, :], ytmp, ALU.add).then_inc(y_read[L], 1)

                def tile(t, first, last):
                    with dve.Fori(0, NPAIR_T - 1) as pr:
                        pair(NPAIR_T * t + pr)
                    if not last:
                        hold(dve, hT_ps[L], t + 1)
                        prep(t + 1, slice(t + 1, t + 2) if isinstance(t, int) else bass.ds(t + 1, 1))
                    if not first:
                        finish(t - 1)
                    pair(NPAIR_T * t + NPAIR_T - 1, last)
                    if not last:
                        take_h(t + 1)

                tile(0, True, False)
                with dve.Fori(1, NT - 1) as t:
                    tile(t, False, False)
                tile(NT - 1, False, True)
                if L == DEPTH - 1:
                    dve.wait_ge(wfin_in, 16)
                    for t in range(NT - 1):
                        final_norm(t)
                finish(NT - 1)
                mean(NT - 1, NT, L + 1, NT)
                inverse(NT - 1, NT, L + 1, 2)
            final_norm(NT - 1)


def dense_copies(L, evac, ps, modc, a_mix, hT, hcT, kT, kcT, vtok, qT, cs, fT, modb, mod_b=None):
    n = 0

    def bank():
        return ps[:, n % 4, :]

    for k in range(KD):
        evac(n, [hT[:, k, :]], [bank()], [a_mix[:, k, 0:1]], [modc[:, k, 0:1]])
        n += 1
    if L == 0:
        for k2 in range(KD // 2):
            evac(n, [hcT[:, 2 * k2 + i, :] for i in range(2)], [bank()[:, i * CTX:(i + 1) * CTX] for i in range(2)],
                 [a_mix[:, 2 * k2 + i, 1:2] for i in range(2)], [modc[:, 2 * k2 + i, 1:2] for i in range(2)])
            n += 1
        for m in range(KD):
            evac(n, [kT[:, m, :]], [bank()])
            n += 1
            evac(n, [kcT[:, m, :]], [bank()[:, 0:CTX]])
            n += 1
        for half in range(2):
            for t in range(NT + NC):
                evac(n, [vtok[:, t, half * BIG:(half + 1) * BIG]], [bank()])
                n += 1
        for m in range(KD):
            evac(n, [qT[:, m, :]], [bank()], scale=DH ** -0.5)
            n += 1
    else:
        for t in range(NT):
            for g in range(4):
                evac(n, [cs[:, t, g, :]], [bank()])
                n += 1
        for j in range(KD):
            evac(n, [fT[:, j, :]], [bank()])
            n += 1
    if mod_b is not None:
        mod_b()
    for v in range(4):
        for half in range(2):
            evac(n, [modb[:, v, half * BIG:(half + 1) * BIG]], [bank()])
            n += 1
    return n


def _bias_index():
    width = 2 * WIN_C - 1
    q, k = np.arange(P), np.arange(WIN)
    at = np.zeros((3, P, WIN), np.int64)
    for v, b in ((0, 0), (1, 1), (2, NT - 1)):
        qc, kc = (b * COLS_T + q // ROWS)[:, None], ((WSTART[b] + k) // ROWS)[None]
        row = (k % ROWS)[None] - (q % ROWS)[:, None] + ROWS - 1
        start = np.clip(qc - WIN_C // 2, 0, GRID_W - WIN_C)
        inside = (kc >= start) & (kc < start + WIN_C)
        at[v] = np.where(inside, row * width + kc - qc + WIN_C - 1, (2 * ROWS - 1) * width)
    return at


def _dft_tables():
    gd = D // 4
    a = 2 * np.pi * (np.outer(np.arange(gd), np.arange(gd)) % gd) / gd
    ch = np.concatenate([np.cos(a), np.sin(a)], 1) / np.sqrt(gd)
    tok = np.arange(SEQ)
    p = (tok % ROWS) * GRID_W + tok // ROWS
    b = 2 * np.pi * (np.outer(p, p) % SEQ) / SEQ
    pos = np.concatenate([np.cos(b), -np.sin(b)], 0) / np.sqrt(SEQ)
    return ch.astype(np.float32), pos.astype(np.float32)


def kernel(x, c, ctx, c_ctx, norm_mix, norm_ffn, w_mod, b_mod, na_w_qkv, na_w_o, na_rpb,
           fno_w_out, peer_w_query, peer_sub_keys, peer_u, peer_v, norm_final):
    import concourse.bacc as _bacc
    from concourse.bass_utils import run_bass_kernel_spmd as _run

    def blocks(v):
        v = np.asarray(v)
        v = v.reshape(v.shape[:-1] + (-1, P))
        return np.moveaxis(v, -1, 0)

    grid = np.asarray(x).reshape(ROWS, GRID_W, D).transpose(1, 0, 2).reshape(SEQ, D)
    cond = np.stack([np.asarray(c).reshape(D), np.asarray(c_ctx)], 0)
    rpb = np.asarray(na_rpb)[0]
    table = np.full((HEADS, rpb[0].size + 1), -1e30, np.float32)
    table[:, :-1] = rpb.reshape(HEADS, -1)
    table = table[:, _bias_index()]
    ch, pos = _dft_tables()
    u, v = np.asarray(peer_u), np.asarray(peer_v)
    arrays = {
        "x": grid, "cT": blocks(cond).transpose(0, 2, 1), "ctx_in": np.asarray(ctx)[0],
        "normT": blocks(np.concatenate([np.asarray(norm_mix), np.asarray(norm_ffn)], 0)),
        "w_mod": w_mod, "bmodT": blocks(b_mod), "w_qkv": np.asarray(na_w_qkv)[0], "w_o": np.asarray(na_w_o)[0],
        "bias_in": table.transpose(1, 2, 0, 3),
        "w_fno": np.asarray(fno_w_out)[0], "w_query": peer_w_query,
        "keysT": np.asarray(peer_sub_keys).transpose(3, 0, 1, 2),
        "peer_u0": u[0], "peer_u1": u[1], "peer_v0": v[0], "peer_v1": v[1],
        "norm_fin": np.broadcast_to(np.asarray(norm_final), (P, D)),
        "dft_ch": ch, "dft_pos": pos, "ident_in": np.eye(P, dtype=np.float32),
        "iota_in": np.concatenate([np.broadcast_to(np.arange(TOPK), (P, TOPK)),
                                   np.repeat(np.eye(2), DH, 0)], 1).astype(np.float32),
    }
    nc = _bacc.Bacc("TRN2", target_bir_lowering=False, num_devices=1)
    args = {}
    for name in list(arrays):
        arrays[name] = np.ascontiguousarray(arrays[name])
        args[name] = nc.dram_tensor(name, arrays[name].shape, mybir.dt.from_np(arrays[name].dtype),
                                    kind="ExternalInput").ap()
    out = nc.dram_tensor("out", (SEQ, D), F32, kind="ExternalOutput").ap()
    build(nc, out=out, **args)
    r = _run(nc, [arrays], core_ids=[0])
    got = np.asarray(r.results[0]["out"])
    return np.ascontiguousarray(got.reshape(GRID_W, ROWS, D).transpose(1, 0, 2)).reshape(1, SEQ, D)
```

```python
from contextlib import ExitStack

import numpy as np
import concourse.bass as bass
from concourse import mybir

ALU = mybir.AluOpType
ACT = mybir.ActivationFunctionType
AX = mybir.AxisListType
F32 = mybir.dt.float32
U32 = mybir.dt.uint32

P = 128
D = 1024
KD = D // P
SEQ = 512
NT = SEQ // P
CTX = 256
NC = CTX // P
GRID_W = 64
ROWS = SEQ // GRID_W
HEADS = 16
PAIRS = HEADS // 2
DH = D // HEADS
WIN_C = 16
COLS_T = P // ROWS
WIN = 256
DEPTH = 2
N_MOD = 6
MODB = N_MOD * KD
PH = 8
NKEY = 128
TOPK = 16
G = 8
NPAIR_T = PH // 2
KSTEPS = 12
DFT_N = 2 * P + 1
EPS = 1e-6
NEG = -3.0e38
BIG = 512
SLOTS = 4
WSTART = [min(max(P * b - WIN // 4, 0), SEQ - WIN) for b in range(NT)]
VARIANT = [0, 1, 1, 2]


def hold(eng, sem, value):
    eng.wait_ge(sem, value)
    eng.nop(nofuse=True)


class Count:

    def __init__(self, eng, sem, base=0):
        self.eng, self.sem, self.base, self.n = eng, sem, base, 0

    def sig(self, ins):
        self.n += 1
        ins.then_inc(self.sem, 1)

    def wait(self):
        if isinstance(self.base, int):
            self.eng.wait_ge(self.sem, self.base + self.n)
        else:
            hold(self.eng, self.sem, self.base + self.n)

    def step(self, ins):
        self.sig(ins)
        self.wait()


def build(nc, x, cT, ctx_in, normT, w_mod, bmodT, w_qkv, w_o, bias_in, w_fno, w_query, keysT,
          peer_u0, peer_u1, peer_v0, peer_v1, norm_fin, dft_ch, dft_pos, ident_in, iota_in, out):
    peer_u, peer_v = [peer_u0, peer_u1], [peer_v0, peer_v1]
    with ExitStack() as ctx:
        def sb(name, shape, dt=F32):
            return ctx.enter_context(nc.sbuf_tensor(name, shape, dt))

        def sem(name):
            return ctx.enter_context(nc.semaphore(name))

        r1 = sb("r1", [P, 16384])
        r2 = sb("r2", [P, 16384])
        r3 = sb("r3", [P, 6144])
        r5 = sb("r5", [P, 4096])
        xres = sb("xres", [P, NT, D])
        modb = sb("modb", [P, 4, D])
        AF, SHF, GF, GM = range(4)

        ring = r1[:, :].rearrange("p (s k n) -> p s k n", s=SLOTS, k=KD)
        urows = r1[:, 0:G * D].rearrange("p (g d) -> p g d", g=G)
        vrows = r1[:, G * D:2 * G * D].rearrange("p (g d) -> p g d", g=G)
        scratch = r1[:, 8192:16384]
        qfix = [scratch[:, 0:128], scratch[:, 128:256]]
        p_mid = [scratch[:, 256 + 640 * i:256 + 640 * (i + 1)] for i in range(2)]
        p_edge = [scratch[:, 1536 + 512 * i:1536 + 512 * (i + 1)] for i in range(2)]
        pT = [scratch[:, 2560 + 640 * i:2560 + 640 * (i + 1)] for i in range(2)]
        qpair = scratch[:, 3840:3968]
        attn = scratch[:, 4096:5120]
        attnT = scratch[:, 5120:6144].rearrange("p (k n) -> p k n", k=KD)
        otmp = scratch[:, 6144:7168]
        sqj = scratch[:, 7168:8192]
        macc = [modb[:, 0, 512 * i:512 * (i + 1)] for i in range(2)]
        arow = [modb[0:2, 1, 512 * i:512 * (i + 1)] for i in range(2)]
        hT = r2[:, 0:4096].rearrange("p (k n) -> p k n", k=KD)
        hcT = r2[:, 4096:6144].rearrange("p (k n) -> p k n", k=KD)
        qT = r2[:, 6144:10240].rearrange("p (k n) -> p k n", k=KD)
        kT = r2[:, 10240:14336].rearrange("p (k n) -> p k n", k=KD)
        kcT = r2[:, 14336:16384].rearrange("p (k n) -> p k n", k=KD)
        vtok = r3[:, :].rearrange("p (t n) -> p t n", t=NT + NC)
        xctx = vtok[:, NT:NT + NC, :]
        xn = r5[:, :].rearrange("p (t n) -> p t n", t=NT)
        bias_a = r5[:, :].rearrange("p (h n) -> p h n", h=HEADS)
        bias_b = r2[:, 0:4096].rearrange("p (h n) -> p h n", h=HEADS)
        bias = [bias_a, bias_b, bias_a]
        cs = r2[:, 4096:8192].rearrange("p (t g n) -> p t g n", t=NT, g=4)
        fT = r2[:, 12288:16384].rearrange("p (k n) -> p k n", k=KD)
        xn1 = r2[:, 12288:16384].rearrange("p (t n) -> p t n", t=NT)
        dft_pos_sb = r2[:, 8192:12288].rearrange("p (k n) -> p k n", k=KD)
        dft_ch_sb = r3[:, 4608:4608 + 2 * DFT_N].rearrange("p (k n) -> p k n", k=2)
        c128 = r3[:, 4096:4096 + NT * 4].rearrange("p (t g) -> p t g", t=NT)
        f128 = r3[0:4, 5376:5888]
        w_plus = r1[:, 4096:8192].rearrange("p (h g n) -> p h g n", h=2, g=4)
        wq = r2[:, :].rearrange("p (c k n) -> p c k n", c=4, k=KD)
        hx_next, hx_cur = r5[:, 0:1024], r5[:, 1024:2048]
        hxT = r5[:, 2048:3072].rearrange("p (k n) -> p k n", k=KD)
        ytmp = r5[:, 3072:4096]
        otmps, sqjs = [otmp, ytmp], [sqj, r3[:, 3072:4096]]
        diag = r3[:, 0:1024].rearrange("p (g n) -> p g n", g=G)
        q_sb = r3[:, 1024:1280]
        qT_sb = r3[:, 1280:1536].rearrange("p (a n) -> p a n", a=2)
        wk = r3[:, 1536:1792].rearrange("p (a n) -> p a n", a=2)
        cand = r3[:, 1792:2048]
        cand2 = r3[:, 2048:2304]
        onehot = r3[:, 2304:2816]
        topv = r3[:, 2816:2848].rearrange("p (a n) -> p a n", a=2)
        tab = r3[:, 2848:2880].rearrange("p (a n) -> p a n", a=2)
        tops = r3[:, 2880:2896]

        ident = sb("ident", [P, P])
        ones = sb("ones", [P, P])
        iota16 = sb("iota16", [P, TOPK + 4])
        keys = sb("keys", [P, DEPTH, 2, NKEY])
        craw = sb("craw", [P, KD, 2])
        silu = sb("silu", [P, KD, 2])
        norms = sb("norms", [P, 2 * DEPTH, KD])
        bmod = sb("bmod", [P, DEPTH, MODB])
        modc = [sb(f"modc{L}", [P, MODB, 2 - L]) for L in range(DEPTH)]
        a_mix = [sb(f"a_mix{L}", [P, KD, 2 - L]) for L in range(DEPTH)]
        a_ffn = [sb(f"a_ffn{L}", [P, KD]) for L in range(DEPTH)]
        ss = sb("ss", [P, NT + NC])
        rstd = sb("rstd", [P, NT + NC])
        nmx = sb("nmx", [P, 2])
        esum = sb("esum", [P, HEADS])
        einv = sb("einv", [P, HEADS])
        ixu = sb("ixu", [P, 2, TOPK], U32)
        pos = sb("pos", [P, TOPK], U32)
        poshl = sb("poshl", [P, TOPK, 2], U32)
        idx = [sb(f"idx{i}", [P, TOPK], U32) for i in range(2)]
        gate_e = [sb(f"gate_e{i}", [P, TOPK]) for i in range(2)]
        gate_r = [sb(f"gate_r{i}", [P, 1]) for i in range(2)]
        expert = sb("expert", [P, TOPK])
        gsum = sb("gsum", [P, 1])
        gneg = sb("gneg", [P, 1])
        pre = sb("pre", [P, 2, G])
        gel = sb("gel", [P, 2, G])
        wgt = sb("wgt", [P, 2, G])
        ps = ctx.enter_context(nc.psum_tensor("ps", [P, 8, 512], F32))

        s_small = sem("s_small")
        s_x = sem("s_x")
        s_ctxin = sem("s_ctxin")
        s_bias = [sem(f"s_bias{v}") for v in range(3)]
        s_out = sem("s_out")
        wa_in = [sem(f"wa_in{i}") for i in range(4)]
        wp_in = [sem(f"wp_in{i}") for i in range(2)]
        wm_in = [sem(f"wm_in{i}") for i in range(2)]
        wf_in = [sem(f"wf_in{i}") for i in range(4)]
        wq_in = [[sem(f"wq_in{L}_{i}") for i in range(4)] for L in range(DEPTH)]
        wfin_in = sem("wfin_in")
        f128_in = sem("f128_in")
        wc_ok = sem("wc_ok")
        s_ones = sem("s_ones")
        s_silu = sem("s_silu")
        sq_done = [sem(f"sq_done{L}") for L in range(DEPTH + 1)]
        var_ok = [sem(f"var_ok{L}") for L in range(DEPTH + 1)]
        std_ok = [sem(f"std_ok{L}") for L in range(DEPTH + 1)]
        rstd_ok = [sem(f"rstd_ok{L}") for L in range(DEPTH + 1)]
        xn_ok = [sem(f"xn_ok{L}") for L in range(DEPTH)]
        a_ps = sem("a_ps")
        arow_ok = sem("arow_ok")
        acol_ps = sem("acol_ps")
        macc_c = sem("macc_c")
        macc_ok = sem("macc_ok")
        mcol_ps = sem("mcol_ps")
        mod_ok = [sem(f"mod_ok{L}") for L in range(DEPTH)]
        dg_ok = [sem(f"dg_ok{L}") for L in range(DEPTH)]
        job = [sem(f"job{L}") for L in range(DEPTH)]
        ev_act = [sem(f"ev_act{L}") for L in range(DEPTH)]
        ev_dve = [sem(f"ev_dve{L}") for L in range(DEPTH)]
        dchain = [sem(f"dchain{L}") for L in range(DEPTH)]
        o_ps = [sem(f"o_ps{L}") for L in range(DEPTH)]
        x_ok = [sem(f"x_ok{L}") for L in range(DEPTH)]
        s_pads = sem("s_pads")
        bias_used = sem("bias_used")
        qp_ok = sem("qp_ok")
        qf_ok = [sem(f"qf_ok{i}") for i in range(2)]
        sc_ps = [sem(f"sc_ps{i}") for i in range(2)]
        lat_ok = [sem(f"lat_ok{i}") for i in range(2)]
        nmx_ok = [sem(f"nmx_ok{i}") for i in range(2)]
        exp_ok = [sem(f"exp_ok{i}") for i in range(2)]
        pt_ps = [sem(f"pt_ps{i}") for i in range(2)]
        pt_act = [sem(f"pt_act{i}") for i in range(2)]
        pt_dve = [sem(f"pt_dve{i}") for i in range(2)]
        pv_ok = [sem(f"pv_ok{i}") for i in range(2)]
        at_chain = sem("at_chain")
        at_ok = sem("at_ok")
        atT_ps = sem("atT_ps")
        atT_ok = sem("atT_ok")
        u_in = [sem(f"u_in{i}") for i in range(G)]
        v_in = [sem(f"v_in{i}") for i in range(G)]
        u_free = [sem(f"u_free{L}") for L in range(DEPTH)]
        v_free = [sem(f"v_free{L}") for L in range(DEPTH)]
        gel_ok = [sem(f"gel_ok{L}") for L in range(DEPTH)]
        w_ok = [sem(f"w_ok{L}") for L in range(DEPTH)]
        dg_in = [sem(f"dg_in{L}") for L in range(DEPTH)]
        q_ps = [sem(f"q_ps{L}") for L in range(DEPTH)]
        q_ok = [sem(f"q_ok{L}") for L in range(DEPTH)]
        qT_ps = [sem(f"qT_ps{L}") for L in range(DEPTH)]
        qT_ok = [sem(f"qT_ok{L}") for L in range(DEPTH)]
        s_ps = [sem(f"s_ps{L}") for L in range(DEPTH)]
        s_read = [sem(f"s_read{L}") for L in range(DEPTH)]
        tk = [sem(f"tk{L}") for L in range(DEPTH)]
        idx_ok = [sem(f"idx_ok{L}") for L in range(DEPTH)]
        top_ok = [sem(f"top_ok{L}") for L in range(DEPTH)]
        gexp_ok = [sem(f"gexp_ok{L}") for L in range(DEPTH)]
        hn_chain = [sem(f"hn_chain{L}") for L in range(DEPTH)]
        hn_ok = [sem(f"hn_ok{L}") for L in range(DEPTH)]
        hT_ps = [sem(f"hT_ps{L}") for L in range(DEPTH)]
        hT_ok = [sem(f"hT_ok{L}") for L in range(DEPTH)]
        hc_ok = [sem(f"hc_ok{L}") for L in range(DEPTH)]
        y_ok = [sem(f"y_ok{L}") for L in range(DEPTH)]
        y_read = [sem(f"y_read{L}") for L in range(DEPTH)]
        fchain = [sem(f"fchain{L}") for L in range(DEPTH)]
        f_out = sem("f_out")

        NITEM = NT * PH
        NGRP = 2 * NITEM
        NSMALL = 6
        CH_A = 4
        NMACC = DEPTH * 2 * N_MOD - CH_A
        JOB_H, JOB_K, JOB_V, JOB_Q = 12, 16, 2 * (NT + NC), 8
        sums_after, m = {}, 0
        for i in range(JOB_H, JOB_H + JOB_K + JOB_V + JOB_Q, 2):
            num = 2 if i >= JOB_H + JOB_K and i % 4 == 0 else 1
            sums_after[i] = list(range(m, min(m + num, NMACC)))
            m += num
        assert m >= NMACC
        USED = [20, 28, 34, 40, 44, 48]
        JOB_M1, JOB_H1, JOB_C1 = 6, 8, 12
        POS1 = JOB_M1 + JOB_H1 + JOB_C1 + 2 + 4
        WHO = ["va" * 28, "a" * (JOB_M1 + JOB_H1 + JOB_C1) + "va" + "a" * (4 + 9 + 2)]
        JOB_BANK = [[0, 1, 2, 3], [2, 3, 6, 7]]

        def copied(l, i, who=None):
            return WHO[l][:i + 1].count(who or WHO[l][i])

        OUT_BANK = [[6, 6, 6, 0], [0, 4, 0, 6]]

        VORD = [AF, SHF, GM, GF]

        def out_of(l, i):
            return ps[:, JOB_BANK[l][i % 4], :]

        def copies_0(evac, before_vectors):
            n = 0
            for k in range(KD):
                evac(0, n, [hT[:, k, :]], [out_of(0, n)], [a_mix[0][:, k, 0:1]], [modc[0][:, k, 0:1]])
                n += 1
            for k2 in range(KD // 2):
                evac(0, n, [hcT[:, 2 * k2 + i, :] for i in range(2)],
                     [out_of(0, n)[:, i * CTX:(i + 1) * CTX] for i in range(2)],
                     [a_mix[0][:, 2 * k2 + i, 1:2] for i in range(2)], [modc[0][:, 2 * k2 + i, 1:2] for i in range(2)])
                n += 1
            for m in range(KD):
                evac(0, n, [kT[:, m, :]], [out_of(0, n)])
                evac(0, n + 1, [kcT[:, m, :]], [out_of(0, n + 1)[:, 0:CTX]])
                n += 2
            for half in range(2):
                for t in range(NT + NC):
                    evac(0, n, [vtok[:, t, half * BIG:(half + 1) * BIG]], [out_of(0, n)])
                    n += 1
            for m in range(KD):
                evac(0, n, [qT[:, m, :]], [out_of(0, n)], scale=DH ** -0.5)
                n += 1
            before_vectors()
            for v in range(4):
                n = vector_copies(evac, 0, n, v)

        def vector_copies(evac, l, n, v):
            for half in range(2):
                evac(l, n, [modb[:, VORD[v], half * BIG:(half + 1) * BIG]], [out_of(l, n)])
                n += 1
            return n

        def copies_1_vectors(evac):
            for v in range(3):
                vector_copies(evac, 1, 2 * v, v)

        def copies_1_turned(evac):
            w = (NT - 1) * P
            for k in range(KD):
                evac(1, JOB_M1 + k, [hT[:, k, 0:w]], [out_of(1, JOB_M1 + k)[:, 0:w]],
                     [a_mix[1][:, k, 0:1]], [modc[1][:, k, 0:1]])

        def channel_copies(evac, n, t):
            for g in range(4):
                evac(1, n + g, [cs[:, t, g, :], c128[:, t, g:g + 1]],
                     [out_of(1, n + g)[:, 0:2 * P], out_of(1, n + g)[:, 2 * P:DFT_N]])

        def copies_1_channel(evac):
            for t in range(NT - 1):
                channel_copies(evac, JOB_M1 + JOB_H1 + 4 * t, t)

        def copies_1_last(evac, with_weights):
            n = JOB_M1 + JOB_H1 + JOB_C1
            for a in range(2):
                evac(1, n, [hT[:, 4 * a + k, (NT - 1) * P:] for k in range(4)],
                     [out_of(1, n)[:, k * P:(k + 1) * P] for k in range(4)],
                     [a_mix[1][:, 4 * a + k, 0:1] for k in range(4)], [modc[1][:, 4 * a + k, 0:1] for k in range(4)])
                n += 1
            with_weights()
            channel_copies(evac, n, NT - 1)
            n += 4
            for g in range(4):
                evac(1, n, [fT[:, 2 * g + 1, :]], [out_of(1, n)])
                n += 1
            evac(1, n, [f128], [out_of(1, n)[0:4, :]])
            n += 1
            for g in range(4):
                evac(1, n, [fT[:, 2 * g, :]], [out_of(1, n)])
                n += 1
            vector_copies(evac, 1, n, 3)

        block = ctx.enter_context(nc.Block())

        @block.sync
        def _(sp):
            sp.dma_start(ident[:], ident_in).then_inc(s_small, 16)
            sp.dma_start(craw[:], cT).then_inc(s_small, 16)
            sp.dma_start(norms[:], normT).then_inc(s_small, 16)
            sp.dma_start(bmod[:], bmodT).then_inc(s_small, 16)
            sp.dma_start(iota16[:], iota_in).then_inc(s_small, 16)
            sp.dma_start(keys[:], keysT).then_inc(s_small, 16)
            def cols(w, c):
                return w.rearrange("(k p) n -> p k n", p=P)[:, :, c * BIG:(c + 1) * BIG]

            for i in range(CH_A):
                sp.dma_start(ring[:, i, :, :], cols(w_mod[0], i)).then_inc(wa_in[i], 16)
                if i == 0:
                    for t in range(NT):
                        sp.dma_start(xres[:, t, :], x[t * P:(t + 1) * P, :]).then_inc(s_x, 16)
                if i == 1:
                    for t in range(NC):
                        sp.dma_start(xctx[:, t, :], ctx_in[t * P:(t + 1) * P, :]).then_inc(s_ctxin, 16)

            def ring_chunk(i, src):
                if i < 2:
                    sp.wait_ge(a_ps, i + 1)
                else:
                    sp.wait_ge(job[0], USED[i - 2])
                sp.dma_start(ring[:, i % 2, :, :], src).then_inc(wp_in[i % 2], 16)

            def bias_load(v):
                sp.dma_start(bias[v], bias_in[v]).then_inc(s_bias[v], 16)

            ring_chunk(0, cols(w_qkv, 2))
            ring_chunk(1, cols(w_qkv, 3))
            sp.wait_ge(job[0], JOB_H)
            bias_load(0)
            ring_chunk(2, cols(w_qkv, 4))
            ring_chunk(3, cols(w_qkv, 5))
            ring_chunk(4, cols(w_qkv, 0))
            ring_chunk(5, cols(w_qkv, 1))
            ring_chunk(6, cols(w_o, 0))
            ring_chunk(7, cols(w_o, 1))
            bias_load(1)
            sp.wait_ge(bias_used, 1)
            bias_load(2)
            sp.wait_ge(bias_used, 3)
            for L in range(DEPTH):
                if L:
                    sp.wait_ge(s_ps[0], NITEM)
                    sp.dma_start(dft_ch_sb, dft_ch.rearrange("(k p) n -> p k n", p=P)).then_inc(wf_in[0], 16)
                    sp.dma_start(dft_pos_sb, dft_pos.rearrange("(k p) n -> p k n", p=P)).then_inc(wf_in[1], 16)
                    sp.wait_ge(v_free[0], (NGRP + 1) * G)
                    for i in range(2):
                        sp.dma_start(ring[:, 2 + i, :, :], cols(w_fno, i)).then_inc(wf_in[2 + i], 16)
                for c4 in range(4):
                    if L == 0 and c4 == 1:
                        sp.wait_ge(at_ok, NT)
                    if L == 1:
                        if c4 == 0:
                            sp.wait_ge(job[L], POS1)
                            sp.wait_ge(ev_act[L], copied(L, POS1 + 4))
                            for g in range(4):
                                sp.dma_start(fT[0:1, 2 * g + 1, :], f128[g:g + 1, :]).then_inc(f128_in, 16)
                        elif c4 == 1:
                            sp.wait_ge(job[L], POS1 + 9)
                        elif c4 == 3:
                            sp.wait_ge(o_ps[L], 2 * NT)
                    sp.dma_start(wq[:, c4, :, :], cols(w_query[L], c4)).then_inc(wq_in[L][c4], 16)
            sp.wait_ge(hT_ps[1], NT)
            sp.wait_ge(hc_ok[1], NT)
            sp.dma_start(hx_next, norm_fin).then_inc(wfin_in, 16)
            for t in range(NT):
                sp.wait_ge(f_out, t + 1)
                sp.dma_start(out[t * P:(t + 1) * P, :], xres[:, t, :]).then_inc(s_out, 16)
            sp.wait_ge(s_out, 16 * NT)

        @block.gpsimd
        def _(pool):
            pool.memset(ones[:], 1.0).then_inc(s_ones, 1)
            for m in range(NMACC):
                if m < 2:
                    pool.wait_ge(a_ps, CH_A)
                else:
                    pool.wait_ge(macc_ok, m - 1)
                L, i = (0, CH_A + m) if m < 2 * N_MOD - CH_A else (1, m - 2 * N_MOD + CH_A)
                pool.dma_start(ring[:, 2 + m % 2, :, :],
                               w_mod[L].rearrange("(k p) n -> p k n", p=P)[:, :, i * BIG:(i + 1) * BIG]
                               ).then_inc(wm_in[m % 2], 16)
            pool.wait_ge(macc_ok, NMACC)
            for i in range(2):
                ins = pool.memset(p_mid[i], 0.0)
            ins.then_inc(s_pads, 1)
            pool.wait_ge(ev_dve[0], (JOB_H + JOB_K + JOB_V + JOB_Q) // 2)
            pool.wait_ge(ev_act[0], (JOB_H + JOB_K + JOB_V + JOB_Q) // 2)
            for b in range(NT):
                def qcopy(j, nn, first=False):
                    if not first:
                        hold(pool, qf_ok[1], nn)
                    pool.tensor_copy(qpair, qT[:, j, b * P:(b + 1) * P]).then_inc(qp_ok, 1)
                    hold(pool, qp_ok, nn + 1)
                    for hh in range(2):
                        if not first:
                            hold(pool, sc_ps[hh], nn)
                        pool.tensor_scalar(qfix[hh], qpair, iota16[:, TOPK + hh:TOPK + hh + 1],
                                           None, ALU.mult).then_inc(qf_ok[hh], 1)

                qcopy(0, PAIRS * b, first=(b == 0))
                with pool.Fori(1, PAIRS) as j:
                    qcopy(j, j + PAIRS * b)

            for L in range(DEPTH):
                def gather(table, rows, b, g8, par, arrived):
                    pool.indirect_dma_start(out=rows[:, b, :], out_offset=None, in_=table,
                                            in_offset=bass.IndirectOffsetOnAxis(ap=idx[par][:, g8 + b:g8 + b + 1],
                                                                                axis=0)).then_inc(arrived[b], 16)

                def u_group(grp, off, par, first=False):
                    for b in range(G):
                        if first and b == 0 and L == 0:
                            pool.wait_ge(o_ps[L], 2 * NT - 1)
                        if first and b == G // 2:
                            pool.wait_ge(o_ps[L], 2 * NT)
                        if b % 4 == 0:
                            hold(pool, u_free[L], G * grp + b + 4)
                        gather(peer_u[L], urows, b, off * G, par, u_in)

                def v_group(grp, off, par):
                    for b in range(G):
                        if b % 4 == 0:
                            hold(pool, v_free[L], G * grp + b + 4)
                        gather(peer_v[L], vrows, b, off * G, par, v_in)

                def pair(m, first):
                    for par in range(2):
                        hold(pool, idx_ok[L], 2 * m + par + 1)
                        u_group(4 * m + 2 * par, 0, par, first and par == 0)
                        if not (first and par == 0):
                            v_group(4 * m + 2 * par - 1, 1, 1 - par)
                        u_group(4 * m + 2 * par + 1, 1, par)
                        if first and par == 0:
                            pool.wait_ge(x_ok[L], NT)
                            pool.wait_ge(sq_done[L], NT + (NC if L == 0 else 0) + NT)
                        v_group(4 * m + 2 * par, 0, par)

                pair(0, True)
                with pool.Fori(1, NITEM // 2) as m:
                    pair(m, False)
                v_group(NGRP - 1, 1, 1)

        @block.tensor
        def _(pe):
            pe.wait_ge(s_small, 16 * NSMALL)
            pe.wait_ge(s_ones, 1)
            pe.wait_ge(s_silu, 1)
            n = [0] * DEPTH
            for L in range(DEPTH):
                def bank(l):
                    i = n[l]
                    if i >= 4:
                        pe.wait_ge((ev_dve if WHO[l][i - 4] == "v" else ev_act)[l], copied(l, i - 4))
                    return ps[:, JOB_BANK[l][i % 4], :]

                def done(l, ins):
                    ins.then_inc(job[l], 1)
                    n[l] += 1
                    if l == 0:
                        for m in sums_after.get(n[0] - 4, []):
                            mod_cols(m)

                def all_copied(l):
                    if copied(l, n[l] - 1, "v"):
                        pe.wait_ge(ev_dve[l], copied(l, n[l] - 1, "v"))
                    pe.wait_ge(ev_act[l], copied(l, n[l] - 1, "a"))

                def mod_cols(m):
                    pe.wait_ge(macc_ok, m + 1)
                    for blk in range(4):
                        at = 2 * 4 * CH_A + 4 * m + blk
                        ins = pe.matmul(ps[:, 7, at:at + 1], macc[m % 2][:, blk * P:(blk + 1) * P], ones[:, 0:1],
                                        start=True, stop=True)
                    ins.then_inc(mcol_ps, 1)

                def ring_wait(i):
                    pe.wait_ge(wp_in[i % 2], 16 * (i // 2 + 1))
                    return ring[:, i % 2, :, :]

                def broadcast(l, v, row):
                    pe.wait_ge(dg_ok[l], v + 1)
                    for half in range(2):
                        dst = bank(l)
                        done(l, pe.matmul(dst, ones[:], modb[:, row, half * 512:(half + 1) * 512], start=True, stop=True))

                def channel_dft(t):
                    pe.wait_ge(wf_in[0], 16)
                    pe.wait_ge(wf_in[1], 16)
                    for g in range(4):
                        dst = bank(1)
                        for kk in range(2):
                            ins = pe.matmul(dst[:, 0:DFT_N], hT[:, 2 * g + kk, t * P:(t + 1) * P], dft_ch_sb[:, kk, :],
                                            start=(kk == 0), stop=(kk == 1))
                        done(1, ins)

                if L == 0:
                    def turn_row(i):
                        pe.wait_ge(arow_ok, i + 1)
                        for blk in range(4):
                            j = 4 * i + blk
                            ins = pe.transpose(ps[:, 7, 2 * j:2 * j + 2], arow[i % 2][:, blk * P:(blk + 1) * P],
                                               ident[0:2, 0:2])
                        ins.then_inc(acol_ps, 1)

                    for i in range(CH_A):
                        pe.wait_ge(wa_in[i], 16)
                        for k in range(KD):
                            ins = pe.matmul(ps[0:2, 4 + i % 2, :], silu[:, k, :], ring[:, i, k, :],
                                            start=(k == 0), stop=(k == KD - 1))
                        ins.then_inc(a_ps, 1)
                        if i:
                            turn_row(i - 1)
                    turn_row(CH_A - 1)
                else:
                    pe.wait_ge(hT_ok[L - 1], 2 * NT)
                pe.wait_ge(xn_ok[L], NT + (NC if L == 0 else 0))
                if L:
                    pe.wait_ge(y_ok[L - 1], NT + 1)
                if L == 0:
                    for k in range(KD):
                        dst = bank(0)
                        for t in range(NT):
                            ins = pe.transpose(dst[:, t * P:(t + 1) * P], xn[:, t, k * P:(k + 1) * P], ident[:])
                        done(0, ins)
                    for k2 in range(KD // 2):
                        dst = bank(0)
                        for kk in range(2):
                            for t in range(NC):
                                k = 2 * k2 + kk
                                ins = pe.transpose(dst[:, (2 * kk + t) * P:(2 * kk + t + 1) * P],
                                                   xctx[:, t, k * P:(k + 1) * P], ident[:])
                        done(0, ins)
                    all_copied(0)
                    c = 0
                    for i in range(2):
                        w = ring_wait(c)
                        for blk in range(4):
                            for src, width in ((hT, SEQ), (hcT, CTX)):
                                dst = bank(0)
                                for k in range(KD):
                                    ins = pe.matmul(dst[:, 0:width], w[:, k, blk * P:(blk + 1) * P], src[:, k, :],
                                                    start=(k == 0), stop=(k == KD - 1))
                                done(0, ins)
                        c += 1
                    for i in range(2):
                        w = ring_wait(c)
                        for t in range(NT + NC):
                            dst = bank(0)
                            for k in range(KD):
                                lhs = hT[:, k, t * P:(t + 1) * P] if t < NT else hcT[:, k, (t - NT) * P:(t - NT + 1) * P]
                                ins = pe.matmul(dst, lhs, w[:, k, :], start=(k == 0), stop=(k == KD - 1))
                            done(0, ins)
                        c += 1
                    for i in range(2):
                        w = ring_wait(c)
                        for blk in range(4):
                            dst = bank(0)
                            for k in range(KD):
                                ins = pe.matmul(dst, w[:, k, blk * P:(blk + 1) * P], hT[:, k, :],
                                                start=(k == 0), stop=(k == KD - 1))
                            done(0, ins)
                        c += 1
                    for m in sums_after[JOB_H + JOB_K + JOB_V + JOB_Q - 2]:
                        mod_cols(m)
                    for v in range(4):
                        broadcast(0, v, VORD[v])
                else:
                    for a in range(2):
                        dst = bank(1)
                        for kk in range(4):
                            ins = pe.transpose(dst[:, kk * P:(kk + 1) * P],
                                               xn1[:, NT - 1, (4 * a + kk) * P:(4 * a + kk + 1) * P], ident[:])
                        done(1, ins)
                    all_copied(1)
                    channel_dft(NT - 1)
                    all_copied(1)
                    w = dft_pos_sb
                    for g in range(4):
                        dst = bank(1)
                        for t in range(NT):
                            ins = pe.matmul(dst, cs[:, t, g, P:2 * P], w[:, NT + t, :], start=(t == 0), stop=(t == NT - 1))
                        done(1, ins)
                    dst = bank(1)
                    for t in range(NT):
                        ins = pe.matmul(dst[0:4, :], c128[:, t, :], w[:, t, :], start=(t == 0), stop=(t == NT - 1))
                    done(1, ins)
                    for g in range(4):
                        dst = bank(1)
                        for t in range(NT):
                            ins = pe.matmul(dst, cs[:, t, g, 0:P], w[:, t, :], start=(t == 0), stop=(t == NT - 1))
                        done(1, ins)
                    broadcast(1, 3, VORD[3])
                all_copied(L)

                if L == 0:
                    wout = [ring_wait(6), ring_wait(7)]
                    w_out = lambda half, k: wout[half][:, k, :]
                else:
                    pe.wait_ge(wf_in[2], 16)
                    pe.wait_ge(wf_in[3], 16)
                    pe.wait_ge(wc_ok, 1)
                    pe.wait_ge(f128_in, 16 * 4)
                    w_out = lambda half, k: ring[:, 2 + half, k, :] if k % 2 else w_plus[:, half, k // 2, :]

                def out_proj(t, half, lhs):
                    for k in range(KD):
                        ins = pe.matmul(ps[:, OUT_BANK[L][t] + half, :], lhs(k), w_out(half, k),
                                        start=(k == 0), stop=(k == KD - 1))
                    ins.then_inc(o_ps[L], 1)

                def turn_h(nt):
                    pe.wait_ge(hn_ok[L], nt + 1)
                    for k in range(KD):
                        ins = pe.transpose(ps[:, 6 + k // 4, (k % 4) * P:(k % 4 + 1) * P],
                                           hx_next[:, k * P:(k + 1) * P], ident[:])
                    ins.then_inc(hT_ps[L], 1)

                def head_scores(chunk, i, par, first=False):
                    if not first:
                        pe.wait_ge(q_ok[L], i)
                    for k in range(KD):
                        ins = pe.matmul(ps[:, 2, 0:256], hxT[:, k, :], wq[:, chunk, k, par * 256:(par + 1) * 256],
                                        start=(k == 0), stop=(k == KD - 1))
                    ins.then_inc(q_ps[L], 1)
                    pe.wait_ge(q_ok[L], i + 1)
                    for a in range(2):
                        ins = pe.transpose(ps[:, 3, a * P:(a + 1) * P], q_sb[:, a * P:(a + 1) * P], ident[:])
                    ins.then_inc(qT_ps[L], 1)
                    pe.wait_ge(qT_ok[L], i + 1)
                    pe.wait_ge(s_read[L], i + 1)
                    for a in range(2):
                        ins = pe.matmul(ps[:, 4 + par, a * P:(a + 1) * P], qT_sb[:, a, :], keys[:, L, a, :],
                                        start=True, stop=True)
                    ins.then_inc(s_ps[L], 1)

                def first_scores():
                    pe.wait_ge(hT_ok[L], 2)
                    pe.wait_ge(wq_in[L][0], 16)
                    pe.wait_ge(x_ok[L], NT - 1 if L == 0 else 2)
                    head_scores(0, 0, 0, first=True)

                if L == 0:
                    pe.wait_ge(s_pads, 1)

                    def scores(b, j, hh, nn):
                        hold(pe, qf_ok[hh], nn + 1)
                        pe.matmul(ps[:, hh, 0:WIN], qfix[hh], kT[:, j, WSTART[b]:WSTART[b] + WIN], start=True, stop=True)
                        pe.matmul(ps[:, hh, WIN:WIN + CTX], qfix[hh], kcT[:, j, :],
                                  start=True, stop=True).then_inc(sc_ps[hh], 1)

                    def turn(b, hh, nn):
                        prob = (p_mid if VARIANT[b] == 1 else p_edge)[hh]
                        pe.wait_ge(exp_ok[hh], nn + 1)
                        if VARIANT[b] == 1:
                            pe.transpose(ps[:, 4 + hh, 0:P], prob[:, 4 * P:5 * P], ident[:])
                        for i in range(4):
                            ins = pe.transpose(ps[:, 2 + hh, i * P:(i + 1) * P], prob[:, i * P:(i + 1) * P], ident[:])
                        ins.then_inc(pt_ps[hh], 1)

                    def values(b, j, hh, nn):
                        first = WSTART[b] // P
                        tiles = list(range(first, first + (3 if VARIANT[b] == 1 else 2))) + [NT, NT + 1]
                        hold(pe, pt_act[hh], nn + 1)
                        if VARIANT[b] == 1:
                            pe.wait_ge(pt_dve[hh], nn - PAIRS + 1)
                        dst = ps[:, 6:8, :].rearrange("p a n -> p (a n)")
                        for i, tile in enumerate(tiles):
                            ins = pe.matmul(dst[:, bass.ds((2 * j + hh) * DH, DH)], pT[hh][:, i * P:(i + 1) * P],
                                            vtok[:, tile, bass.ds((2 * j + hh) * DH, DH)],
                                            start=(i == 0), stop=(i == len(tiles) - 1))
                        ins.then_inc(pv_ok[hh], 1)

                    scores(0, 0, 0, 0)
                    scores(0, 0, 1, 0)
                    turn(0, 0, 0)
                    scores(0, 1, 0, 1)
                    for b in range(NT):
                        base = b * PAIRS

                        def heads(j, first=False, last=False):
                            turn(b, 1, j + base)
                            scores(b, j + 1, 1, j + 1 + base)
                            if first:
                                pe.wait_ge(x_ok[L], b)
                            values(b, j, 0, j + base)
                            turn(b, 0, j + 1 + base)
                            if not last:
                                scores(b, j + 2, 0, j + 2 + base)
                            values(b, j, 1, j + base)

                        heads(0, first=b > 0)
                        with pe.Fori(1, PAIRS - 2) as j:
                            heads(j)
                        heads(PAIRS - 2, last=True)
                        last = base + PAIRS - 1
                        turn(b, 1, last)
                        values(b, PAIRS - 1, 0, last)
                        values(b, PAIRS - 1, 1, last)
                        if b < NT - 1:
                            scores(b + 1, 0, 0, last + 1)
                            scores(b + 1, 0, 1, last + 1)
                        pe.wait_ge(at_ok, b + 1)
                        for k in range(KD):
                            ins = pe.transpose(ps[:, 3 + 2 * (k // 4), (k % 4) * P:(k % 4 + 1) * P],
                                               attn[:, k * P:(k + 1) * P], ident[:])
                        ins.then_inc(atT_ps, 1)
                        if b < NT - 1:
                            turn(b + 1, 0, last + 1)
                            scores(b + 1, 1, 0, last + 2)
                        else:
                            turn_h(0)
                        pe.wait_ge(atT_ok, b + 1)
                        if b == NT - 1:
                            first_scores()
                        for half in range(2):
                            out_proj(b, half, lambda k: attnT[:, k, :])
                else:
                    for t in range(NT):
                        if t == 2:
                            turn_h(0)
                            pe.wait_ge(x_ok[L], 1)
                        if t == 3:
                            first_scores()
                        for half in range(2):
                            out_proj(t, half, lambda k: fT[:, k, t * P:(t + 1) * P])

                def add_rows(grp, start):
                    for b in range(G):
                        pe.wait_ge(dg_in[L], G * grp + b + 1)
                        pe.wait_ge(v_in[b], 16 * grp + 16 * (NGRP * L + 1))
                        for half in range(2):
                            ins = pe.matmul(ps[:, half, :], diag[:, b, :], vrows[:, b, half * 512:(half + 1) * 512],
                                            start=(start and b == 0), stop=False, skip_group_check=True)
                        ins.then_inc(v_free[L], 1)

                def pair(m, next_chunk, tile_start, chain=True):
                    ahead = L == 0 and not chain
                    if ahead:
                        pe.wait_ge(qT_ok[0], NITEM)
                        pe.wait_ge(hT_ok[0], 2 * NT)
                        for v in range(3):
                            broadcast(1, v, VORD[v])
                        pe.wait_ge(xn_ok[1], NT - 1)
                        for k in range(KD):
                            dst = bank(1)
                            for t in range(NT - 1):
                                ins = pe.transpose(dst[:, t * P:(t + 1) * P], xn1[:, t, k * P:(k + 1) * P], ident[:])
                            done(1, ins)
                    for par in range(2):
                        add_rows(4 * m + 2 * par, tile_start and par == 0)
                        if chain:
                            head_scores(next_chunk, 2 * m + par + 2, par)
                        if ahead and par == 0:
                            all_copied(1)
                            for t in range(NT - 1):
                                channel_dft(t)
                        add_rows(4 * m + 2 * par + 1, False)

                def tile(t, last, chunks=False):
                    hold(pe, y_ok[L], t + 1)
                    if chunks:
                        pe.wait_ge(wq_in[L][1], 16)
                    pair(NPAIR_T * t, 1, True)
                    if chunks:
                        for c4 in range(2, 4):
                            pe.wait_ge(wq_in[L][c4], 16)
                    with pe.Fori(1, NPAIR_T - 1) as pr:
                        pair(NPAIR_T * t + pr, pr + 1, False)
                    if not last:
                        turn_h(t + 1)
                        hold(pe, hT_ok[L], 2 * t + 4)
                    pair(NPAIR_T * t + NPAIR_T - 1, 0, False, chain=not last)

                pe.sem_inc(v_free[L], G)
                head_scores(0, 1, 1)
                pe.wait_ge(x_ok[L], NT)
                tile(0, False, chunks=True)
                with pe.Fori(1, NT - 1) as t:
                    tile(t, False)
                tile(NT - 1, True)

        @block.scalar
        def _(act):
            act.wait_ge(s_small, 16 * NSMALL)
            act.activation(silu[:], craw[:], ACT.Silu).then_inc(s_silu, 1)
            for L in range(DEPTH):
                tiles = [xres[:, t, :] for t in range(NT)] + ([xctx[:, t, :] for t in range(NC)] if L == 0 else [])

                def square(t, n):
                    act.wait_ge(sq_done[L], n)
                    act.activation(sqjs[L], xres[:, t, :], ACT.Square, accum_out=ss[:, t:t + 1]).then_inc(sq_done[L], 1)

                def root(t0, t1, k):
                    act.wait_ge(var_ok[L], k)
                    act.activation(rstd[:, t0:t1], ss[:, t0:t1], ACT.Sqrt).then_inc(std_ok[L], 1)

                if L == 0:
                    for i, src in enumerate(tiles):
                        if i == 0:
                            act.wait_ge(s_x, 16 * NT)
                        if i == NT:
                            act.wait_ge(s_ctxin, 16 * NC)
                        act.activation(xn[:, 0, :], src, ACT.Square,
                                       accum_out=ss[:, i:i + 1]).then_inc(sq_done[L], 1)
                        act.wait_ge(sq_done[L], i + 1)
                    root(0, len(tiles), 1)
                    act.wait_ge(rstd_ok[L], 1)
                    for i, src in enumerate(tiles):
                        dst = xn[:, i, :] if i < NT else src
                        act.activation(dst, src, ACT.Copy, scale=rstd[:, i:i + 1]).then_inc(xn_ok[L], 1)
                else:
                    act.wait_ge(rstd_ok[L], 2)
                    act.activation(xn1[:, NT - 1, :], xres[:, NT - 1, :], ACT.Copy,
                                   scale=rstd[:, NT - 1:NT]).then_inc(xn_ok[L], 1)

                def evac(l, i, outs, ins_, scales=None, shifts=None, scale=1.0):
                    if WHO[l][i] != "a":
                        return
                    act.wait_ge(job[l], i + 1)
                    for q, (o, s) in enumerate(zip(outs, ins_)):
                        if scales is not None:
                            ins = act.activation(o, s, ACT.Identity, bias=shifts[q], scale=scales[q])
                        else:
                            ins = act.activation(o, s, ACT.Copy, scale=scale)
                    ins.then_inc(ev_act[l], 1)

                def turned_h(nt):
                    act.wait_ge(hT_ps[L], nt + 1)
                    for a in range(2):
                        act.activation(hxT[:, 4 * a:4 * a + 4, :], ps[:, 6 + a, :].rearrange("p (k n) -> p k n", k=4),
                                       ACT.Copy).then_inc(hT_ok[L], 1)

                act.wait_ge(mod_ok[L], 1)
                if L == 0:
                    copies_0(evac, lambda: None)
                else:
                    copies_1_last(evac, lambda: None)

                if L == 0:
                    def soft(b, hh, nn, h):
                        prob = p_edge[hh].rearrange("p (a n) -> p a n", a=2)
                        if VARIANT[b] == 1:
                            prob = p_mid[hh].rearrange("p (a n) -> p a n", a=2)[:, :, 64:64 + WIN]
                        act.wait_ge(nmx_ok[hh], nn + 1)
                        act.activation(prob, ps[:, hh, :].rearrange("p (a n) -> p a n", a=2), ACT.Exp,
                                       bias=nmx[:, hh:hh + 1], accum_out=esum[:, h]).then_inc(exp_ok[hh], 1)

                    def turned(hh, nn):
                        act.wait_ge(pt_ps[hh], nn + 1)
                        act.activation(pT[hh][:, 0:512], ps[:, 2 + hh, :], ACT.Copy).then_inc(pt_act[hh], 1)

                    act.wait_ge(s_pads, 1)
                    for b in range(NT):
                        base = b * PAIRS
                        if b == 0:
                            soft(0, 0, 0, slice(0, 1))
                            soft(0, 1, 0, slice(1, 2))
                        turned(0, base)
                        if b:
                            act.wait_ge(x_ok[L], b)
                            square(b - 1, len(tiles) + b - 1)
                        with act.Fori(0, PAIRS - 1) as j:
                            turned(1, j + base)
                            soft(b, 0, j + 1 + base, bass.ds(2 * j + 2, 1))
                            turned(0, j + 1 + base)
                            soft(b, 1, j + 1 + base, bass.ds(2 * j + 3, 1))
                        turned(1, base + PAIRS - 1)
                        if b == NT - 1:
                            root(0, 1, 2)
                        if b < NT - 1:
                            act.wait_ge(at_chain, b + 1)
                            soft(b + 1, 0, base + PAIRS, slice(0, 1))
                            soft(b + 1, 1, base + PAIRS, slice(1, 2))
                        act.wait_ge(atT_ps, b + 1)
                        for a in range(2):
                            ins = act.activation(attnT[:, 4 * a:4 * a + 4, :],
                                                 ps[:, 3 + 2 * a, :].rearrange("p (k n) -> p k n", k=4), ACT.Copy)
                        ins.then_inc(atT_ok, 1)
                else:
                    for t in range(NT - 1):
                        act.wait_ge(x_ok[L], t + 1)
                        square(t, len(tiles) + t)
                        if t == 0:
                            root(0, 1, 3)
                        if t == 0:
                            turned_h(0)
                def query_copies(i):
                    act.wait_ge(q_ps[L], i + 1)
                    act.activation(q_sb, ps[:, 2, 0:256], ACT.Copy).then_inc(q_ok[L], 1)
                    act.wait_ge(qT_ps[L], i + 1)
                    act.activation(qT_sb, ps[:, 3, 0:256].rearrange("p (a n) -> p a n", a=2),
                                   ACT.Copy).then_inc(qT_ok[L], 1)

                def gate_exp(i, par):
                    act.wait_ge(top_ok[L], i + 1)
                    act.activation(gate_e[par][:], tops, ACT.Exp, bias=gneg[:],
                                   accum_out=gsum[:]).then_inc(gexp_ok[L], 1)

                def gelu(grp, gp):
                    act.wait_ge(u_free[L], G * grp + 2 * G)
                    act.activation(gel[:, gp, :], pre[:, gp, :], ACT.Gelu).then_inc(gel_ok[L], 1)

                def diags(grp, gp):
                    act.wait_ge(w_ok[L], grp + 1)
                    for b in range(G):
                        act.wait_ge(v_free[L], G * grp + b + 1)
                        act.activation(diag[:, b, :], ident[:], ACT.Copy,
                                       scale=wgt[:, gp, b:b + 1]).then_inc(dg_in[L], 1)

                def next_square(t):
                    if t:
                        act.wait_ge(sq_done[L + 1], t)
                    act.activation(sqjs[1], xres[:, t, :], ACT.Square,
                                   accum_out=ss[:, t:t + 1]).then_inc(sq_done[L + 1], 1)

                def next_root(t0, t1, k):
                    act.wait_ge(var_ok[L + 1], k)
                    act.activation(rstd[:, t0:t1], ss[:, t0:t1], ACT.Sqrt).then_inc(std_ok[L + 1], 1)

                def pair(m, chain=True, last=False):
                    for par in range(2):
                        g0 = 4 * m + 2 * par
                        gelu(g0, 0)
                        if last and par == 0 and L == 0:
                            act.wait_ge(rstd_ok[1], 1)
                            act.wait_ge(s_ps[0], NITEM)
                            for tt in range(NT - 1):
                                act.activation(xn1[:, tt, :], xres[:, tt, :], ACT.Copy,
                                               scale=rstd[:, tt:tt + 1]).then_inc(xn_ok[1], 1)
                        diags(g0, 0)
                        if last and par == 0 and L == 0:
                            copies_1_vectors(evac)
                            copies_1_turned(evac)
                        if chain:
                            query_copies(2 * m + par + 2)
                        gelu(g0 + 1, 1)
                        if not (last and par == 1):
                            gate_exp(2 * m + par + 1, 1 - par)
                        diags(g0 + 1, 1)
                        if last and par == 0 and L == 0:
                            copies_1_channel(evac)

                def tile(t, last):
                    with act.Fori(0, NPAIR_T - 1) as pr:
                        pair(NPAIR_T * t + pr)
                    if not last:
                        turned_h(t + 1)
                    else:
                        act.wait_ge(y_read[L], NT)
                        for tt in range(NT - 1):
                            next_square(tt)
                        next_root(0, NT - 1, 1)
                    pair(NPAIR_T * t + NPAIR_T - 1, chain=not last, last=last)
                    act.wait_ge(v_free[L], G * 2 * PH * (t + 1) + G)
                    act.wait_ge(y_read[L], t + 1)
                    act.activation(ytmp, ps[:, 0:2, :].rearrange("p a n -> p (a n)"), ACT.Copy).then_inc(y_ok[L], 1)

                act.sem_inc(y_ok[L], 1)
                if L == 0:
                    turned_h(0)
                query_copies(0)
                gate_exp(0, 0)
                query_copies(1)
                act.wait_ge(x_ok[L], NT)
                square(NT - 1, len(tiles) + NT - 1)
                root(1, NT, 3 + L)
                tile(0, False)
                with act.Fori(1, NT - 1) as t:
                    tile(t, False)
                tile(NT - 1, True)
                act.wait_ge(y_read[L], NT + 1)
                next_square(NT - 1)
                next_root(NT - 1, NT, 2)

        @block.vector
        def _(dve):
            dve.wait_ge(s_small, 16 * NSMALL)
            for L in range(DEPTH):
                ch = Count(dve, dchain[L])
                nt_ln = NT + (NC if L == 0 else 0)

                def mean(t0, t1, ln, squares):
                    dve.wait_ge(sq_done[ln], squares)
                    dve.tensor_scalar(ss[:, t0:t1], ss[:, t0:t1], 1.0 / D, EPS, ALU.mult, ALU.add).then_inc(var_ok[ln], 1)

                def inverse(t0, t1, ln, k):
                    dve.wait_ge(std_ok[ln], k)
                    dve.reciprocal(rstd[:, t0:t1], rstd[:, t0:t1]).then_inc(rstd_ok[ln], 1)
                    dve.wait_ge(rstd_ok[ln], k)

                if L == 0:
                    mean(0, nt_ln, 0, nt_ln)
                    inverse(0, nt_ln, 0, 1)
                if L == 0:
                    for i in range(CH_A):
                        dve.wait_ge(a_ps, i + 1)
                        if i >= 2:
                            dve.wait_ge(acol_ps, i - 1)
                        dve.tensor_copy(arow[i % 2], ps[0:2, 4 + i % 2, :]).then_inc(arow_ok, 1)
                    nA = 4 * CH_A
                    dve.wait_ge(acol_ps, CH_A)
                    ch.step(dve.tensor_tensor(modc[0][:, 0:nA, :], ps[:, 7, 0:2 * nA].rearrange("p (j n) -> p j n", n=2),
                                              bmod[:, 0, 0:nA].unsqueeze(2).to_broadcast([P, nA, 2]), ALU.add))
                    ch.step(dve.tensor_scalar(a_mix[0][:], modc[0][:, KD:2 * KD, :], 1.0, None, ALU.add))
                    dve.tensor_tensor(a_mix[0][:], a_mix[0][:], norms[:, 0, :].unsqueeze(2).to_broadcast([P, KD, 2]),
                                      ALU.mult).then_inc(mod_ok[L], 1)
                    dve.wait_ge(mod_ok[L], 1)

                mc = Count(dve, macc_c)

                def mod_sum(m):
                    w = ring[:, 2 + m % 2, :, :]
                    dve.wait_ge(wm_in[m % 2], 16 * (m // 2 + 1))
                    if m >= 2:
                        dve.wait_ge(mcol_ps, m - 1)
                    mc.step(dve.tensor_scalar(macc[m % 2], w[:, 0, :], silu[:, 0, 0:1], None, ALU.mult))
                    for k in range(1, KD):
                        ins = dve.scalar_tensor_tensor(macc[m % 2], w[:, k, :], silu[:, k, 0:1], macc[m % 2],
                                                       ALU.mult, ALU.add)
                        if k < KD - 1:
                            mc.step(ins)
                    ins.then_inc(macc_ok, 1)

                def evac(l, i, outs, ins_, scales=None, shifts=None, scale=1.0):
                    if WHO[l][i] != "v":
                        return
                    dve.wait_ge(job[l], i + 1)
                    for q, (o, s) in enumerate(zip(outs, ins_)):
                        if scales is not None:
                            ins = dve.tensor_scalar(o, s, scales[q], shifts[q], ALU.mult, ALU.add)
                        elif scale != 1.0:
                            ins = dve.tensor_scalar(o, s, scale, None, ALU.mult)
                        else:
                            ins = dve.tensor_copy(o, s)
                    ins.then_inc(ev_dve[l], 1)
                    if l == 0:
                        for m in sums_after.get(i, []):
                            mod_sum(m)

                def spread(l, v):
                    row = VORD[v]
                    col = {AF: a_ffn[l][:], SHF: modc[l][:, 3 * KD:4 * KD, 0],
                           GF: modc[l][:, 5 * KD:6 * KD, 0], GM: modc[l][:, 2 * KD:3 * KD, 0]}[row]
                    dve.tensor_tensor(modb[:, row, :].rearrange("p (k n) -> p k n", k=KD),
                                      ident[:, :].unsqueeze(1).to_broadcast([P, KD, P]),
                                      col.unsqueeze(2).to_broadcast([P, KD, P]), ALU.mult).then_inc(dg_ok[l], 1)

                def mod_b():
                    dve.wait_ge(mcol_ps, NMACC)
                    at = 2 * nA
                    ch.step(dve.tensor_tensor(modc[0][:, nA:MODB, 0], ps[:, 7, at:at + MODB - nA],
                                              bmod[:, 0, nA:MODB], ALU.add))
                    at += MODB - nA
                    ch.step(dve.tensor_tensor(modc[1][:, :, 0], ps[:, 7, at:at + MODB], bmod[:, 1, :], ALU.add))
                    for l in range(DEPTH):
                        ch.step(dve.tensor_scalar(a_ffn[l][:], modc[l][:, 4 * KD:5 * KD, 0], 1.0, None, ALU.add))
                        ch.step(dve.tensor_tensor(a_ffn[l][:], a_ffn[l][:], norms[:, DEPTH + l, :], ALU.mult))
                    ch.step(dve.tensor_scalar(a_mix[1][:, :, 0], modc[1][:, KD:2 * KD, 0], 1.0, None, ALU.add))
                    dve.tensor_tensor(a_mix[1][:, :, 0], a_mix[1][:, :, 0], norms[:, 1, :], ALU.mult).then_inc(mod_ok[1], 1)
                    dve.wait_ge(mod_ok[1], 1)
                    for v in range(4):
                        spread(0, v)

                def fno_weights():
                    spread(1, 3)
                    mask = iota16[:, TOPK + 2:TOPK + 3], iota16[:, TOPK + 3:TOPK + 4]
                    for half in range(2):
                        dve.wait_ge(wf_in[2 + half], 16)
                        rows = ring[:, 2 + half, :, :].rearrange("p (g a) n -> p g a n", a=2)
                        ch.step(dve.scalar_tensor_tensor(w_plus[:, half], rows[:, :, 1, :], mask[0], rows[:, :, 0, :],
                                                         ALU.mult, ALU.add))
                        ins = dve.scalar_tensor_tensor(rows[:, :, 1, :], rows[:, :, 0, :], mask[1], rows[:, :, 1, :],
                                                       ALU.mult, ALU.add)
                        if half == 0:
                            ch.step(ins)
                    ins.then_inc(wc_ok, 1)

                if L == 0:
                    copies_0(evac, mod_b)
                else:
                    copies_1_last(evac, fno_weights)
                dve.wait_ge(ev_act[L], WHO[L].count("a"))

                def residual(t):
                    dve.wait_ge(o_ps[L], 2 * t + 2)
                    b0 = OUT_BANK[L][t]
                    ch.step(dve.tensor_tensor(otmps[L], ps[:, b0:b0 + 2, :].rearrange("p a n -> p (a n)"),
                                              modb[:, GM, :], ALU.mult))
                    dve.tensor_tensor(xres[:, t, :], xres[:, t, :], otmps[L], ALU.add).then_inc(x_ok[L], 1)
                    dve.wait_ge(x_ok[L], t + 1)

                def prep(t, col):
                    dve.scalar_tensor_tensor(hx_next, xres[:, t, :], rstd[:, col], modb[:, AF, :],
                                             ALU.mult, ALU.mult).then_inc(hn_chain[L], 1)
                    hold(dve, hn_chain[L], t + 1)
                    dve.tensor_tensor(hx_next, hx_next, modb[:, SHF, :], ALU.add).then_inc(hn_ok[L], 1)

                def take_h(t):
                    hold(dve, hn_ok[L], t + 1)
                    hold(dve, u_free[L], 2 * PH * G * t + G)
                    dve.tensor_copy(hx_cur, hx_next).then_inc(hc_ok[L], 1)
                    hold(dve, hc_ok[L], t + 1)

                def dots(grp, gp):
                    for b in range(G):
                        dve.wait_ge(u_in[b], 16 * grp + 16 * (NGRP * L + 1))
                        dve.tensor_tensor_reduce(urows[:, b, :], urows[:, b, :], hx_cur, 1.0, 0.0, ALU.mult, ALU.add,
                                                 pre[:, gp, b:b + 1]).then_inc(u_free[L], 1)

                def weights(grp, gp, par):
                    hold(dve, gel_ok[L], grp + 1)
                    dve.scalar_tensor_tensor(wgt[:, gp, :], gel[:, gp, :], gate_r[par][:],
                                             gate_e[par][:, gp * G:(gp + 1) * G],
                                             ALU.mult, ALU.mult).then_inc(w_ok[L], 1)

                def halves(i, par):
                    ct = Count(dve, tk[L], KSTEPS * i)
                    score = [ps[:, 4 + par, a * P:(a + 1) * P] for a in range(2)]
                    hold(dve, s_ps[L], i + 1)
                    dve.max(topv[:, 0, 0:8], score[0])
                    ct.step(dve.max(topv[:, 1, 0:8], score[1]))
                    for a in range(2):
                        dve.match_replace(wk[:, a, :], topv[:, a, 0:8], score[a], NEG)
                    dve.max_index(ixu[:, 0, 0:8], topv[:, 0, 0:8], score[0])
                    dve.max_index(ixu[:, 1, 0:8], topv[:, 1, 0:8], score[1]).then_inc(s_read[L], 1)
                    hold(dve, s_read[L], i + 3)
                    dve.max(topv[:, 0, 8:16], wk[:, 0, :])
                    ct.step(dve.max(topv[:, 1, 8:16], wk[:, 1, :]))
                    dve.max_index(ixu[:, 0, 8:16], topv[:, 0, 8:16], wk[:, 0, :])
                    ct.step(dve.max_index(ixu[:, 1, 8:16], topv[:, 1, 8:16], wk[:, 1, :]))
                    dve.tensor_tensor(cand.rearrange("p (a b) -> p a b", a=TOPK),
                                      topv[:, 0, :].unsqueeze(2).to_broadcast([P, TOPK, TOPK]),
                                      topv[:, 1, :].unsqueeze(1).to_broadcast([P, TOPK, TOPK]), ALU.add)
                    dve.tensor_scalar(tab[:, 0, :], ixu[:, 0, :], float(NKEY), None, ALU.mult)
                    ct.step(dve.tensor_copy(tab[:, 1, :], ixu[:, 1, :]))
                    return ct

                def choose(i, par, ct):
                    ct.step(dve.max(tops[:, 0:8], cand))
                    dve.match_replace(cand2, tops[:, 0:8], cand, NEG)
                    ct.step(dve.max_index(pos[:, 0:8], tops[:, 0:8], cand))
                    dve.tensor_scalar(gneg[:], tops[:, 0:1], -1.0, None, ALU.mult)
                    dve.max(tops[:, 8:16], cand2).then_inc(top_ok[L], 1)
                    hold(dve, top_ok[L], i + 1)
                    ct.step(dve.max_index(pos[:, 8:16], tops[:, 8:16], cand2))
                    dve.tensor_scalar(poshl[:, :, 0], pos[:], 4, None, ALU.logical_shift_right)
                    ct.step(dve.tensor_scalar(poshl[:, :, 1], pos[:], TOPK - 1, None, ALU.bitwise_and))
                    oh = onehot.rearrange("p (k a n) -> p k a n", k=TOPK, a=2)
                    ct.step(dve.tensor_tensor(oh, poshl[:, :, :].unsqueeze(3).to_broadcast([P, TOPK, 2, TOPK]),
                                              iota16[:, 0:TOPK].unsqueeze(1).unsqueeze(1).to_broadcast([P, TOPK, 2, TOPK]),
                                              ALU.is_equal))
                    ct.step(dve.tensor_tensor(oh, oh, tab.unsqueeze(1).to_broadcast([P, TOPK, 2, TOPK]), ALU.mult))
                    if not isinstance(i, int) or i > 0:
                        hold(dve, v_free[L], 2 * G * i - G)
                    ct.step(dve.tensor_reduce(expert[:], onehot.rearrange("p (k n) -> p k n", k=TOPK), AX.X, ALU.add))
                    dve.tensor_copy(idx[par][:], expert[:]).then_inc(idx_ok[L], 1)
                    hold(dve, gexp_ok[L], i + 1)
                    ct.step(dve.reciprocal(gate_r[par][:], gsum[:]))
                    assert ct.n == KSTEPS, ct.n

                def first_h():
                    dve.sem_inc(u_free[L], G)
                    dve.sem_inc(s_read[L], 2)
                    dve.sem_inc(y_read[L], 1)
                    prep(0, slice(0, 1))
                    take_h(0)

                if L == 0:
                    def masked(b, hh, nn, h):
                        hold(dve, sc_ps[hh], nn + 1)
                        dve.tensor_tensor(ps[:, hh, 0:WIN], ps[:, hh, 0:WIN], bias[VARIANT[b]][:, h, :],
                                          ALU.add).then_inc(lat_ok[hh], 1)
                        hold(dve, lat_ok[hh], nn + 1)
                        dve.tensor_reduce(nmx[:, hh:hh + 1], ps[:, hh, :], AX.X, ALU.max,
                                          negate=True).then_inc(nmx_ok[hh], 1)

                    def turned(b, hh, nn):
                        if VARIANT[b] == 1:
                            hold(dve, pt_ps[hh], nn + 1)
                            dve.tensor_copy(pT[hh][:, 512:640], ps[:, 4 + hh, 0:P]).then_inc(pt_dve[hh], 1)

                    dve.wait_ge(s_bias[0], 16)
                    masked(0, 0, 0, slice(0, 1))
                    masked(0, 1, 0, slice(1, 2))
                    for b in range(NT):
                        base = b * PAIRS
                        turned(b, 0, base)
                        with dve.Fori(0, PAIRS - 1) as j:
                            masked(b, 0, j + 1 + base, bass.ds(2 * j + 2, 1))
                            turned(b, 1, j + base)
                            masked(b, 1, j + 1 + base, bass.ds(2 * j + 3, 1))
                            turned(b, 0, j + 1 + base)
                        turned(b, 1, base + PAIRS - 1)
                        if b == NT - 1:
                            mean(0, 1, L, nt_ln + 1)
                        dve.wait_ge(nmx_ok[1], base + PAIRS)
                        dve.sem_inc(bias_used, 1)
                        dve.wait_ge(exp_ok[1], base + PAIRS)
                        dve.reciprocal(einv[:], esum[:]).then_inc(at_chain, 1)
                        dve.wait_ge(at_chain, b + 1)
                        dve.wait_ge(pv_ok[1], base + PAIRS)
                        dve.tensor_tensor(attn.rearrange("p (h n) -> p h n", h=HEADS),
                                          ps[:, 6:8, :].rearrange("p a (h n) -> p (a h) n", h=PAIRS),
                                          einv[:].unsqueeze(2).to_broadcast([P, HEADS, DH]), ALU.mult).then_inc(at_ok, 1)
                        if b < NT - 1:
                            dve.wait_ge(s_bias[VARIANT[b + 1]], 16)
                            masked(b + 1, 0, base + PAIRS, slice(0, 1))
                            masked(b + 1, 1, base + PAIRS, slice(1, 2))
                        if b < NT - 1:
                            residual(b)
                    inverse(0, 1, L, 2)
                    first_h()
                else:
                    residual(0)
                    mean(0, 1, L, nt_ln + 1)
                    inverse(0, 1, L, 3)
                    first_h()
                    residual(1)
                    residual(2)
                choose(0, 0, halves(0, 0))
                residual(NT - 1)
                mean(1, NT, L, nt_ln + NT)
                inverse(1, NT, L, 3 + L)

                def pair(m, last=False):
                    for par in range(2):
                        i = 2 * m + par
                        more = not (last and par == 1)
                        dots(2 * i, 0)
                        if last and par == 0:
                            inverse(0, NT - 1, L + 1, 1)
                        if more:
                            ct = halves(i + 1, 1 - par)
                        weights(2 * i, 0, par)
                        dots(2 * i + 1, 1)
                        if more:
                            choose(i + 1, 1 - par, ct)
                        weights(2 * i + 1, 1, par)

                def final_norm(t):
                    dve.scalar_tensor_tensor(xres[:, t, :], xres[:, t, :], rstd[:, t:t + 1], hx_next, ALU.mult,
                                             ALU.mult).then_inc(f_out, 1)

                def finish(t):
                    hold(dve, y_ok[L], t + 2)
                    dve.tensor_tensor(ytmp, ytmp, modb[:, GF, :], ALU.mult).then_inc(fchain[L], 1)
                    hold(dve, fchain[L], t + 1)
                    dve.tensor_tensor(xres[:, t, :], xres[:, t, :], ytmp, ALU.add).then_inc(y_read[L], 1)

                def tile(t, first, last):
                    with dve.Fori(0, NPAIR_T - 1) as pr:
                        pair(NPAIR_T * t + pr)
                    if not last:
                        hold(dve, hT_ps[L], t + 1)
                        prep(t + 1, slice(t + 1, t + 2) if isinstance(t, int) else bass.ds(t + 1, 1))
                    if not first:
                        finish(t - 1)
                    if last and L == 0:
                        for v in range(3):
                            spread(1, v)
                    if last:
                        mean(0, NT - 1, L + 1, NT - 1)
                    pair(NPAIR_T * t + NPAIR_T - 1, last)
                    if not last:
                        take_h(t + 1)

                tile(0, True, False)
                with dve.Fori(1, NT - 1) as t:
                    tile(t, False, False)
                tile(NT - 1, False, True)
                if L == DEPTH - 1:
                    dve.wait_ge(wfin_in, 16)
                    for t in range(NT - 1):
                        final_norm(t)
                finish(NT - 1)
                dve.wait_ge(y_read[L], NT + 1)
                mean(NT - 1, NT, L + 1, NT)
                inverse(NT - 1, NT, L + 1, 2)
            final_norm(NT - 1)


def _bias_index():
    width = 2 * WIN_C - 1
    q, k = np.arange(P), np.arange(WIN)
    at = np.zeros((3, P, WIN), np.int64)
    for v, b in ((0, 0), (1, 1), (2, NT - 1)):
        qc, kc = (b * COLS_T + q // ROWS)[:, None], ((WSTART[b] + k) // ROWS)[None]
        row = (k % ROWS)[None] - (q % ROWS)[:, None] + ROWS - 1
        start = np.clip(qc - WIN_C // 2, 0, GRID_W - WIN_C)
        inside = (kc >= start) & (kc < start + WIN_C)
        at[v] = np.where(inside, row * width + kc - qc + WIN_C - 1, (2 * ROWS - 1) * width)
    return at


def _dft_tables():
    gd = D // 4
    a = 2 * np.pi * (np.outer(np.arange(gd), np.arange(gd)) % gd) / gd
    ch = np.concatenate([np.cos(a[:, :P]), np.sin(a[:, :P]), np.cos(a[:, P:P + 1])], 1) / np.sqrt(gd)
    tok = np.arange(SEQ)
    p = (tok % ROWS) * GRID_W + tok // ROWS
    b = 2 * np.pi * (np.outer(p, p) % SEQ) / SEQ
    pos = np.concatenate([np.cos(b), np.sin(b)], 0) / np.sqrt(SEQ)
    return ch.astype(np.float32), pos.astype(np.float32)


def kernel(x, c, ctx, c_ctx, norm_mix, norm_ffn, w_mod, b_mod, na_w_qkv, na_w_o, na_rpb,
           fno_w_out, peer_w_query, peer_sub_keys, peer_u, peer_v, norm_final):
    import concourse.bacc as _bacc
    from concourse.bass_utils import run_bass_kernel_spmd as _run

    def blocks(v):
        v = np.asarray(v)
        v = v.reshape(v.shape[:-1] + (-1, P))
        return np.moveaxis(v, -1, 0)

    grid = np.asarray(x).reshape(ROWS, GRID_W, D).transpose(1, 0, 2).reshape(SEQ, D)
    cond = np.stack([np.asarray(c).reshape(D), np.asarray(c_ctx)], 0)
    rpb = np.asarray(na_rpb)[0]
    table = np.full((HEADS, rpb[0].size + 1), -1e30, np.float32)
    table[:, :-1] = rpb.reshape(HEADS, -1)
    table = table[:, _bias_index()]
    ch, pos = _dft_tables()
    half = np.concatenate([np.arange(P), [P], np.arange(2 * P - 1, P, -1)])
    rows = (np.arange(4)[:, None] * 2 * P + half[None]).reshape(-1)
    u, v = np.asarray(peer_u), np.asarray(peer_v)
    arrays = {
        "x": grid, "cT": blocks(cond).transpose(0, 2, 1), "ctx_in": np.asarray(ctx)[0],
        "normT": blocks(np.concatenate([np.asarray(norm_mix), np.asarray(norm_ffn)], 0)),
        "w_mod": w_mod, "bmodT": blocks(b_mod), "w_qkv": np.asarray(na_w_qkv)[0], "w_o": np.asarray(na_w_o)[0],
        "bias_in": table.transpose(1, 2, 0, 3),
        "w_fno": np.asarray(fno_w_out)[0][rows], "w_query": peer_w_query,
        "keysT": np.asarray(peer_sub_keys).transpose(3, 0, 1, 2),
        "peer_u0": u[0], "peer_u1": u[1], "peer_v0": v[0], "peer_v1": v[1],
        "norm_fin": np.broadcast_to(np.asarray(norm_final), (P, D)),
        "dft_ch": ch, "dft_pos": pos, "ident_in": np.eye(P, dtype=np.float32),
        "iota_in": np.concatenate([np.broadcast_to(np.arange(TOPK), (P, TOPK)),
                                   np.repeat(np.eye(2), DH, 0),
                                   np.outer(np.arange(P) > 0, [1, -1])], 1).astype(np.float32),
    }
    nc = _bacc.Bacc("TRN2", target_bir_lowering=False, num_devices=1)
    args = {}
    for name in list(arrays):
        arrays[name] = np.ascontiguousarray(arrays[name])
        args[name] = nc.dram_tensor(name, arrays[name].shape, mybir.dt.from_np(arrays[name].dtype),
                                    kind="ExternalInput").ap()
    out = nc.dram_tensor("out", (SEQ, D), F32, kind="ExternalOutput").ap()
    build(nc, out=out, **args)
    r = _run(nc, [arrays], core_ids=[0])
    got = np.asarray(r.results[0]["out"])
    return np.ascontiguousarray(got.reshape(GRID_W, ROWS, D).transpose(1, 0, 2)).reshape(1, SEQ, D)
```
